# Optimizing a Trainium2 kernel written in Bass

```python
import jax
import jax.numpy as jnp
from jax import lax
import numpy as np

D_MODEL = 1024
BATCH = 1
SEQ = 1024
DEPTH = 1
DEC_BATCH = 1
DEC_SEQ = 64
PAST_LEN = 1024

CHUNK = 64
N_META = 16
MLA_HEADS = 8
MLA_V = D_MODEL // (2 * MLA_HEADS)
MLA_NOPE = MLA_V
MLA_ROPE = MLA_NOPE // 2
MLA_QK = MLA_NOPE + MLA_ROPE
MLA_Q_LORA = D_MODEL // 4
MLA_KV_LORA = D_MODEL // 8
MLA_SCALE = MLA_QK ** -0.5
ROPE_BASE = 10000.0
Q_BLOCK = 128
M_HEADS = 4
M_DV = D_MODEL // (2 * M_HEADS)
M_DK = M_DV // 2
PROJ_NAMES = ('cq', 'ckv', 'kr', 'mq', 'mk', 'mv', 'mi', 'mf', 'mo')
PROJ_WIDTHS = (MLA_Q_LORA, MLA_KV_LORA, MLA_ROPE, M_HEADS * M_DK, M_HEADS * M_DK, M_HEADS * M_DV, M_HEADS, M_HEADS, M_HEADS * M_DV)
PROJ_DIM = MLA_Q_LORA + MLA_KV_LORA + MLA_ROPE + 2 * M_HEADS * M_DK + 2 * M_HEADS * M_DV + 2 * M_HEADS
MIX_DIM = MLA_HEADS * MLA_V + M_HEADS * M_DV
N_GROUPS = 4
E_PER_GROUP = 8
N_EXPERTS = N_GROUPS * E_PER_GROUP
TOP_K = 2
EXPERT_FF = D_MODEL // 2
MOE_BLOCK = 128
EPS = 1e-6

kernel_name = 'hymba_mla_mlstm_hmoe_stream_step'

def rms_norm(x, g):
    xf = x.astype(jnp.float32)
    y = xf * lax.rsqrt(jnp.mean(xf * xf, axis=-1, keepdims=True) + EPS)
    return (y * g.astype(jnp.float32)).astype(x.dtype)

def rope(x, pos):
    half = x.shape[-1] // 2
    inv = ROPE_BASE ** (-jnp.arange(half, dtype=jnp.float32) / half)
    ang = pos.astype(jnp.float32)[:, None] * inv[None, :]
    ang = ang.reshape((1, ang.shape[0]) + (1,) * (x.ndim - 3) + (half,))
    cos, sin = jnp.cos(ang), jnp.sin(ang)
    x1 = x[..., :half].astype(jnp.float32)
    x2 = x[..., half:].astype(jnp.float32)
    return jnp.concatenate([x1 * cos - x2 * sin, x1 * sin + x2 * cos], axis=-1).astype(x.dtype)

def project(x, lp):
    z = jnp.einsum('bld,dp->blp', rms_norm(x, lp['g_attn']), lp['w_in'])
    out, off = {}, 0
    for name, w in zip(PROJ_NAMES, PROJ_WIDTHS):
        out[name] = z[..., off:off + w]
        off += w
    return out

def latent_rows(pr, pos, lp):
    return rms_norm(pr['ckv'], lp['g_ckv']), rope(pr['kr'], pos)

def mla_queries(cq, pos, lp):
    q = jnp.einsum('blr,rhe->blhe', rms_norm(cq, lp['g_cq']), lp['w_uq'])
    q = jnp.concatenate([q[..., :MLA_NOPE], rope(q[..., MLA_NOPE:], pos)], axis=-1)
    return rms_norm(q, lp['g_q'])

def mla_keys_values(ckv, kr, lp):
    kv = jnp.einsum('blc,che->blhe', ckv, lp['w_ukv'])
    kr_h = jnp.broadcast_to(kr[:, :, None, :], kv.shape[:3] + (MLA_ROPE,))
    k = rms_norm(jnp.concatenate([kv[..., :MLA_NOPE], kr_h], axis=-1), lp['g_k'])
    return k, kv[..., MLA_NOPE:]

def attend_block(q, k, v, q_cid, k_cid):
    s = jnp.einsum('bqhe,bkhe->bhqk', q, k).astype(jnp.float32) * MLA_SCALE
    visible = k_cid[None, :] <= q_cid[:, None]
    s = jnp.where(visible[None, None], s, -jnp.inf)
    p = jax.nn.softmax(s, axis=-1).astype(v.dtype)
    return jnp.einsum('bhqk,bkhe->bqhe', p, v)

def attend(q, k, v, q_cid, k_cid):
    b, lq = q.shape[:2]
    if lq <= Q_BLOCK:
        return attend_block(q, k, v, q_cid, k_cid)
    nb = lq // Q_BLOCK
    qb = q.reshape((b, nb, Q_BLOCK) + q.shape[2:]).swapaxes(0, 1)
    cb = q_cid.reshape(nb, Q_BLOCK)
    out = lax.map(lambda a: attend_block(a[0], k, v, a[1], k_cid), (qb, cb))
    return out.swapaxes(0, 1).reshape((b, lq) + out.shape[3:])

def mlstm_zero_state(b, dtype):
    return (jnp.zeros((b, M_HEADS, M_DV, M_DK), dtype), jnp.zeros((b, M_HEADS, M_DK), dtype), jnp.zeros((b, M_HEADS), dtype))

def mlstm_gates(pr, lp):
    b, l = pr['mk'].shape[:2]
    k = pr['mk'].reshape(b, l, M_HEADS, M_DK) * (M_DK ** -0.5)
    v = pr['mv'].reshape(b, l, M_HEADS, M_DV)
    ig = pr['mi'].astype(jnp.float32) + lp['b_igate'].astype(jnp.float32)
    logf = jax.nn.log_sigmoid(pr['mf'].astype(jnp.float32) + lp['b_fgate'].astype(jnp.float32))
    return k, v, ig, logf

def mlstm_state_update(state, k, v, ig, logf):
    c, n, m = state
    k, v = k.astype(jnp.float32), v.astype(jnp.float32)
    mf = m.astype(jnp.float32)
    b = jnp.cumsum(logf, axis=1)
    b_last = b[:, -1]
    log_w = b_last[:, None] - b + ig
    m_new = jnp.maximum(b_last + mf, jnp.max(log_w, axis=1))
    w = jnp.exp(log_w - m_new[:, None])
    decay = jnp.exp(b_last + mf - m_new)
    c_new = decay[..., None, None] * c.astype(jnp.float32) + jnp.einsum('bsh,bshv,bshd->bhvd', w, v, k)
    n_new = decay[..., None] * n.astype(jnp.float32) + jnp.einsum('bsh,bshd->bhd', w, k)
    return (c_new.astype(c.dtype), n_new.astype(n.dtype), m_new.astype(m.dtype))

def mlstm_block(state, q, k, v, ig, logf):
    c, n, m = state
    qf, kf, vf = q.astype(jnp.float32), k.astype(jnp.float32), v.astype(jnp.float32)
    l = q.shape[1]
    b = jnp.cumsum(logf, axis=1)
    causal = jnp.tril(jnp.ones((l, l), dtype=bool))
    log_d = b[:, :, None, :] - b[:, None, :, :] + ig[:, None, :, :]
    log_d = jnp.where(causal[None, :, :, None], log_d, -jnp.inf)
    log_inter = b + m.astype(jnp.float32)[:, None, :]
    m_t = jnp.maximum(log_inter, jnp.max(log_d, axis=2))
    w = jnp.exp(log_d - m_t[:, :, None, :]) * jnp.einsum('bthd,bshd->btsh', qf, kf)
    inter = jnp.exp(log_inter - m_t)
    num = jnp.einsum('btsh,bshv->bthv', w, vf) + inter[..., None] * jnp.einsum('bhvd,bthd->bthv', c.astype(jnp.float32), qf)
    den = jnp.sum(w, axis=2) + inter * jnp.einsum('bhd,bthd->bth', n.astype(jnp.float32), qf)
    h = num / jnp.maximum(jnp.abs(den), jnp.exp(-m_t))[..., None]
    return h, mlstm_state_update(state, k, v, ig, logf)

def mlstm_run(state, q, k, v, ig, logf):
    b, l = q.shape[:2]
    if l <= CHUNK:
        h, state = mlstm_block(state, q, k, v, ig, logf)
        return h.astype(q.dtype), state
    nc = l // CHUNK

    def split(a):
        return a.reshape((b, nc, CHUNK) + a.shape[2:]).swapaxes(0, 1)

    def step(st, xs):
        h, st = mlstm_block(st, *xs)
        return st, h.astype(q.dtype)

    state, hs = lax.scan(step, state, (split(q), split(k), split(v), split(ig), split(logf)))
    return hs.swapaxes(0, 1).reshape((b, l) + hs.shape[3:]), state

def hier_route(xf, lp):
    t = xf.shape[0]
    rows = jnp.arange(t)
    g_logits = (xf @ lp['w_group']).astype(jnp.float32) + lp['b_group'].astype(jnp.float32)
    g_prob = jax.nn.softmax(g_logits, axis=-1)
    g_idx = lax.top_k(g_logits, 1)[1][:, 0]
    e_logits = ((xf @ lp['w_erouter']).astype(jnp.float32) + lp['b_erouter'].astype(jnp.float32)).reshape(t, N_GROUPS, E_PER_GROUP)
    e_sel = e_logits[rows, g_idx]
    e_val, e_idx = lax.top_k(e_sel, TOP_K)
    gate = g_prob[rows, g_idx][:, None] * jax.nn.softmax(e_val, axis=-1)
    return g_idx[:, None] * E_PER_GROUP + e_idx, gate

def moe(h, lp):
    b, l, d = h.shape
    t = b * l
    a = t * TOP_K
    xf = h.reshape(t, d)
    expert, gate = hier_route(xf, lp)
    e_flat = expert.reshape(a)
    order = jnp.argsort(e_flat)
    e_sorted = e_flat[order]
    tok_sorted = (jnp.arange(a) // TOP_K)[order]
    g_sorted = gate.reshape(a)[order].astype(h.dtype)
    counts = jnp.bincount(e_flat, length=N_EXPERTS)
    start = jnp.cumsum(counts) - counts
    padded = (counts + MOE_BLOCK - 1) // MOE_BLOCK * MOE_BLOCK
    pend = jnp.cumsum(padded)
    pstart = pend - padded
    dest = pstart[e_sorted] + jnp.arange(a) - start[e_sorted]
    nb = (a + N_EXPERTS * (MOE_BLOCK - 1)) // MOE_BLOCK + 1
    xs = jnp.zeros((nb * MOE_BLOCK, d), h.dtype).at[dest].set(xf[tok_sorted])
    blk_e = jnp.minimum(jnp.searchsorted(pend, jnp.arange(nb) * MOE_BLOCK, side='right'), N_EXPERTS - 1)

    def expert_block(args):
        xb, e = args
        return (jax.nn.silu(xb @ lp['w1'][e]) * (xb @ lp['w3'][e])) @ lp['w2'][e]

    ys = lax.map(expert_block, (xs.reshape(nb, MOE_BLOCK, d), blk_e)).reshape(nb * MOE_BLOCK, d)
    contrib = ys[dest] * g_sorted[:, None]
    return jnp.zeros((t, d), h.dtype).at[tok_sorted].add(contrib).reshape(b, l, d)

def frame_layer(x, pos, cid, ctx_ckv, ctx_kr, ctx_cid, mstate, lp):
    b, l = x.shape[:2]
    pr = project(x, lp)
    ckv, kr = latent_rows(pr, pos, lp)
    q = mla_queries(pr['cq'], pos, lp)
    k, v = mla_keys_values(jnp.concatenate([ctx_ckv, ckv], axis=1), jnp.concatenate([ctx_kr, kr], axis=1), lp)
    att = attend(q, k, v, cid, jnp.concatenate([ctx_cid, cid]))
    mk, mv, ig, logf = mlstm_gates(pr, lp)
    mq = pr['mq'].reshape(b, l, M_HEADS, M_DK)
    hm, mstate_new = mlstm_run(mstate, mq, mk, mv, ig, logf)
    hm = rms_norm(hm, lp['g_mh']) * jax.nn.sigmoid(pr['mo']).reshape(b, l, M_HEADS, M_DV)
    mix = jnp.concatenate([att.reshape(b, l, MLA_HEADS * MLA_V), hm.reshape(b, l, M_HEADS * M_DV)], axis=-1)
    x = x + jnp.einsum('blm,md->bld', mix, lp['w_out'])
    x = x + moe(rms_norm(x, lp['g_ffn']), lp)
    return x, ckv, kr, mstate_new

def meta_rows_state(meta_h, meta_pos, lp):
    pr = project(meta_h, lp)
    ckv, kr = latent_rows(pr, meta_pos, lp)
    mk, mv, ig, logf = mlstm_gates(pr, lp)
    return ckv, kr, mlstm_state_update(mlstm_zero_state(1, meta_h.dtype), mk, mv, ig, logf)

def setup_inputs(seed: int = 0) -> dict:
    key = jax.random.key(seed)
    ks = jax.random.split(key, 32)

    def nrm(k, shape, scale):
        return jax.random.normal(k, shape, jnp.float32) * scale

    def gain(k, shape):
        return 1.0 + 0.05 * jax.random.normal(k, shape, jnp.float32)

    f_bias = jnp.linspace(3.0, 6.0, M_HEADS, dtype=jnp.float32)[None, :] + nrm(ks[14], (DEPTH, M_HEADS), 0.1)
    return {
        'x_prompt': nrm(ks[0], (BATCH, SEQ, D_MODEL), 1.0),
        'x_sample': nrm(ks[1], (DEC_BATCH, DEC_SEQ, D_MODEL), 1.0),
        'cache_ckv': nrm(ks[2], (DEPTH, DEC_BATCH, PAST_LEN, MLA_KV_LORA), 1.0),
        'cache_krope': nrm(ks[3], (DEPTH, DEC_BATCH, PAST_LEN, MLA_ROPE), 1.0),
        'state_mlstm_c': nrm(ks[4], (DEPTH, DEC_BATCH, M_HEADS, M_DV, M_DK), 0.1),
        'state_mlstm_n': nrm(ks[5], (DEPTH, DEC_BATCH, M_HEADS, M_DK), 0.1),
        'state_mlstm_m': nrm(ks[6], (DEPTH, DEC_BATCH, M_HEADS), 1.0),
        'meta_tokens': nrm(ks[7], (N_META, D_MODEL), 1.0),
        'g_attn': gain(ks[8], (DEPTH, D_MODEL)),
        'w_in': nrm(ks[9], (DEPTH, D_MODEL, PROJ_DIM), D_MODEL ** -0.5),
        'g_cq': gain(ks[10], (DEPTH, MLA_Q_LORA)),
        'w_uq': nrm(ks[11], (DEPTH, MLA_Q_LORA, MLA_HEADS, MLA_QK), MLA_Q_LORA ** -0.5),
        'g_ckv': gain(ks[12], (DEPTH, MLA_KV_LORA)),
        'w_ukv': nrm(ks[13], (DEPTH, MLA_KV_LORA, MLA_HEADS, MLA_NOPE + MLA_V), MLA_KV_LORA ** -0.5),
        'g_q': gain(ks[15], (DEPTH, MLA_QK)),
        'g_k': gain(ks[16], (DEPTH, MLA_QK)),
        'b_igate': nrm(ks[17], (DEPTH, M_HEADS), 0.1),
        'b_fgate': f_bias,
        'g_mh': gain(ks[18], (DEPTH, M_HEADS, M_DV)),
        'w_out': nrm(ks[19], (DEPTH, MIX_DIM, D_MODEL), MIX_DIM ** -0.5),
        'g_ffn': gain(ks[20], (DEPTH, D_MODEL)),
        'w_group': nrm(ks[21], (DEPTH, D_MODEL, N_GROUPS), D_MODEL ** -0.5),
        'b_group': nrm(ks[22], (DEPTH, N_GROUPS), 0.01),
        'w_erouter': nrm(ks[23], (DEPTH, D_MODEL, N_EXPERTS), D_MODEL ** -0.5),
        'b_erouter': nrm(ks[24], (DEPTH, N_EXPERTS), 0.01),
        'w1': nrm(ks[25], (DEPTH, N_EXPERTS, D_MODEL, EXPERT_FF), D_MODEL ** -0.5),
        'w3': nrm(ks[26], (DEPTH, N_EXPERTS, D_MODEL, EXPERT_FF), D_MODEL ** -0.5),
        'w2': nrm(ks[27], (DEPTH, N_EXPERTS, EXPERT_FF, D_MODEL), EXPERT_FF ** -0.5),
    }

def reference(x_prompt, x_sample, cache_ckv, cache_krope, state_mlstm_c, state_mlstm_n, state_mlstm_m,
              meta_tokens, g_attn, w_in, g_cq, w_uq, g_ckv, w_ukv, g_q, g_k, b_igate, b_fgate, g_mh,
              w_out, g_ffn, w_group, b_group, w_erouter, b_erouter, w1, w3, w2):
    bp, seq = x_prompt.shape[:2]
    bs, dec_seq = x_sample.shape[:2]
    past = cache_ckv.shape[2]
    meta_pos = jnp.arange(N_META) - N_META
    meta_cid = jnp.full((N_META,), -1, dtype=jnp.int32)
    p_pos = jnp.arange(seq)
    p_cid = (p_pos // CHUNK).astype(jnp.int32)
    s_pos = past + jnp.arange(dec_seq)
    s_cid = (s_pos // CHUNK).astype(jnp.int32)
    c_cid = (jnp.arange(past) // CHUNK).astype(jnp.int32)

    def bcast(a, b):
        return jnp.broadcast_to(a, (b,) + a.shape[1:])

    meta_h = meta_tokens[None]
    xp, xs = x_prompt, x_sample
    ckv_p, kr_p, c_p, n_p, m_p = [], [], [], [], []
    ckv_s, kr_s, c_s, n_s, m_s = [], [], [], [], []
    for layer in range(DEPTH):
        lp = {'g_attn': g_attn[layer], 'w_in': w_in[layer], 'g_cq': g_cq[layer], 'w_uq': w_uq[layer],
              'g_ckv': g_ckv[layer], 'w_ukv': w_ukv[layer], 'g_q': g_q[layer], 'g_k': g_k[layer],
              'b_igate': b_igate[layer], 'b_fgate': b_fgate[layer], 'g_mh': g_mh[layer], 'w_out': w_out[layer],
              'g_ffn': g_ffn[layer], 'w_group': w_group[layer], 'b_group': b_group[layer],
              'w_erouter': w_erouter[layer], 'b_erouter': b_erouter[layer],
              'w1': w1[layer], 'w3': w3[layer], 'w2': w2[layer]}
        if layer + 1 < DEPTH:
            dt = meta_h.dtype
            meta_h, m_ckv, m_kr, m_state = frame_layer(
                meta_h, meta_pos, meta_cid, jnp.zeros((1, 0, MLA_KV_LORA), dt), jnp.zeros((1, 0, MLA_ROPE), dt),
                jnp.zeros((0,), jnp.int32), mlstm_zero_state(1, dt), lp)
        else:
            m_ckv, m_kr, m_state = meta_rows_state(meta_h, meta_pos, lp)
        xp, pc, pk, pst = frame_layer(xp, p_pos, p_cid, bcast(m_ckv, bp), bcast(m_kr, bp), meta_cid,
                                      (bcast(m_state[0], bp), bcast(m_state[1], bp), bcast(m_state[2], bp)), lp)
        xs, sc, sk, sst = frame_layer(xs, s_pos, s_cid,
                                      jnp.concatenate([bcast(m_ckv, bs), cache_ckv[layer]], axis=1),
                                      jnp.concatenate([bcast(m_kr, bs), cache_krope[layer]], axis=1),
                                      jnp.concatenate([meta_cid, c_cid]),
                                      (state_mlstm_c[layer], state_mlstm_n[layer], state_mlstm_m[layer]), lp)
        ckv_p.append(jnp.concatenate([bcast(m_ckv, bp), pc], axis=1))
        kr_p.append(jnp.concatenate([bcast(m_kr, bp), pk], axis=1))
        c_p.append(pst[0])
        n_p.append(pst[1])
        m_p.append(pst[2])
        ckv_s.append(sc)
        kr_s.append(sk)
        c_s.append(sst[0])
        n_s.append(sst[1])
        m_s.append(sst[2])
    new_ckv_prompt = jnp.stack(ckv_p)
    new_krope_prompt = jnp.stack(kr_p)
    new_c_prompt = jnp.stack(c_p)
    new_n_prompt = jnp.stack(n_p)
    new_m_prompt = jnp.stack(m_p)
    new_ckv_sample = jnp.stack(ckv_s)
    new_krope_sample = jnp.stack(kr_s)
    new_c_sample = jnp.stack(c_s)
    new_n_sample = jnp.stack(n_s)
    new_m_sample = jnp.stack(m_s)
    return (xp, xs, new_ckv_prompt, new_krope_prompt, new_c_prompt, new_n_prompt, new_m_prompt,
            new_ckv_sample, new_krope_sample, new_c_sample, new_n_sample, new_m_sample)


_drawn_inputs = setup_inputs


def setup_inputs(seed=0):
    import zlib

    import numpy as np

    out = dict(_drawn_inputs(seed))
    spreads = {}
    factors = {'g_cq': 4.324, 'g_q': 4.408, 'g_k': 6.519, 'b_erouter': 3.251}
    for name, (base, spread) in spreads.items():
        noise = np.random.default_rng([zlib.crc32(name.encode()), seed]).standard_normal(out[name].shape)
        drawn = base * np.exp(spread * noise) if base else spread * noise
        out[name] = jnp.asarray(drawn.astype(out[name].dtype))
    for name, factor in factors.items():
        out[name] = (out[name] * factor).astype(out[name].dtype)
    return out
```

```python
from contextlib import ExitStack

import numpy as np

import concourse.bass as bass
from concourse import mybir

F32 = mybir.dt.float32
U32 = mybir.dt.uint32
I32 = mybir.dt.int32
ALU = mybir.AluOpType
ACT = mybir.ActivationFunctionType
AX = mybir.AxisListType.X

P = 128
D = 1024
KD = D // P
SEQ, DEC, META, PAST = 1024, 64, 16, 1024
NT = 1 + SEQ // P
NC = PAST // P
ROWS = NT * P
CH = 64
NCH = ROWS // CH
HA, NOPE, ROPE, VD = 8, 64, 32, 64
QK = NOPE + ROPE
QL, KL = 256, 128
HM, DK, DV = 4, 64, 128
CAUG = DV + 1
EPS = 1e-6
NG, EG = 4, 8
NE = NG * EG
FF = 512
KF = FF // P
Z_CQ, Z_CKV, Z_KR, Z_GATE, Z_MQ, Z_MK, Z_MV, Z_MO = 0, 256, 384, 416, 424, 680, 936, 1448
ZW = 1960
Z_CHUNKS = [(0, 424), (424, 936), (936, 1448), (1448, 1960)]
SLOTS = NT + 1
BANK = 512
NEG = -1.0e30
TOKENS = SEQ + DEC
MAX_OVER = (2 * TOKENS - 2) // P
NBLK = NE + MAX_OVER
NSLOT = NBLK * P
NOWHERE = 1.0e6


def constants():
    c = {}
    c["ident"] = np.eye(P, dtype=np.float32)
    s, t = np.meshgrid(np.arange(P), np.arange(P), indexing="ij")
    c["chunk_mask"] = np.where((s // CH == t // CH) & (s <= t), 0.0, NEG).astype(np.float32)
    c["before"] = (s < t).astype(np.float32)
    pos = np.zeros(ROWS)
    pos[:DEC] = PAST + np.arange(DEC)
    pos[DEC:DEC + META] = np.arange(META) - META
    pos[P:] = np.arange(SEQ)
    half = ROPE // 2
    inv = np.float32(10000.0) ** (-np.arange(half, dtype=np.float32) / np.float32(half))
    ang = pos.astype(np.float32)[:, None] * inv[None, :].astype(np.float32)
    cos, sin = np.cos(ang).astype(np.float32), np.sin(ang).astype(np.float32)
    table = np.concatenate([cos, cos, -sin, sin], axis=1).reshape(NT, P, 2 * ROPE)
    c["rope"] = np.ascontiguousarray(table.transpose(1, 0, 2).reshape(P, NT * 2 * ROPE))
    keep = np.ones(ROWS, np.float32)
    keep[DEC + META:P] = 0.0
    start = (np.arange(ROWS) % CH == 0)
    rows = [keep, np.where(keep > 0, 0.0, NEG), np.where(start, 0.0, 1.0), np.where(start, 3 * NEG, 0.0)]
    c["gate_rows"] = np.broadcast_to(np.stack(rows).astype(np.float32)[None], (HM, 4, ROWS)).reshape(HM, 4 * ROWS).copy()
    sel = np.zeros((HM, HM, P), np.float32)
    for h in range(HM):
        sel[h, h] = 1.0
    c["pick_head"] = sel.reshape(HM, HM * P)
    ro = np.zeros((P, 5 * NE + 2 * NT + 2 * NT + NT), np.float32)
    ro[:, 0:NE] = np.arange(NE)
    ro[:, NE:2 * NE] = np.arange(NE) * P
    ro[:, 2 * NE:2 * NE + MAX_OVER] = np.arange(MAX_OVER)
    tok = np.arange(NT)[None, :] * P + np.arange(P)[:, None]
    at = 5 * NE
    ro[:, at:at + NT] = tok
    ro[:, at + NT:at + 2 * NT] = tok
    ro[DEC:, at + 2 * NT] = NOWHERE
    c["route_rows"] = ro
    empty = np.zeros((NSLOT, 4), np.float32)
    empty[:, 1] = NOWHERE
    c["empty_slots"] = empty
    return c


CONSTS = constants()
INS = {
    "x_rows": (ROWS, D), "cache_ckv": (PAST, KL), "cache_kr": (PAST, ROPE), "state_c": (DK, HM * CAUG),
    "state_m": (HM, 1), "g_attn": (P, KD), "w_in": (D, ZW), "g_cq": (P, QL // P), "w_uq": (QL, HA * QK),
    "g_ckv": (1, KL), "w_ukv": (KL, 2 * HA * VD), "g_q": (QK, 1), "g_k": (QK, 1), "b_gate": (HM, 2),
    "g_mh": (1, HM * DV), "w_out": (D, D), "g_ffn": (1, D), "w_route": (D, NG + NE), "b_route": (1, NG + NE),
    "w1": (NE, D, FF), "w3": (NE, D, FF), "w2": (NE, FF, D),
}
OUTS = {
    "y": (ROWS, D), "ckv": (ROWS, KL), "krope": (ROWS, ROPE), "c_prompt": (DK, HM * CAUG),
    "c_sample": (DK, HM * CAUG), "m_both": (2, HM, 1),
}


def key_blocks(n):
    if n == 0:
        return [(i * P, 2 + i, 0, P) for i in range(NC)] + [(NC * P, 0, 0, DEC + META)]
    return [(i * P, 1 + i, 0, P) for i in range(n)] + [(n * P, 0, DEC, META)]


def pe_fills():
    order = []
    for c in range(NC + 1):
        if c < NC:
            order += [("ckvT", c), ("kn", c), ("v", c)]
        if c >= 1:
            order += [("kTa", c - 1), ("kTb", c - 1)]
    for n in range(-1, NT + 1):
        for h in range(HA):
            order += [key for key in filler(n, h) if key[0] not in NO_BANK]
            if 0 <= n < NT:
                order += [("pT", n, h, g) for g in range((len(key_blocks(n)) + 3) // 4)]
        order += [key for key in filler(n, HA) if key[0] not in NO_BANK]
    fills, used = {}, [0, 0, 0, 0]
    for i, key in enumerate(order):
        assert key not in fills, key
        fills[key] = (i % 4, used[i % 4])
        used[i % 4] += 1
    return fills, used


def filler(n, h):
    now, nxt, old = 0 <= n < NT, n + 1 < NT, n >= 1
    m = NC + n + 1
    return {
        0: [("mxa", n - 1), ("mxb", n - 1)] * old + [("gt", n), ("nm", n)] * now,
        1: [("o0", n - 1)] * old + [("cqT", n + 1)] * nxt,
        2: [("o1", n - 1)] * old + [("qbT", n), ("kbT", n)] * now + [("ckvT", m)] * nxt,
        3: [("qkm", n), ("ua", n), ("ub", n)] * now + [("q0", n + 1), ("q1", n + 1)] * nxt + [("xnorm", n - 1)] * old,
        4: [("kn", m), ("v", m)] * nxt + [("ia", n), ("na", n)] * now + [("qsum", n + 1)] * nxt,
        5: [("ib", n), ("nb", n)] * now + [("xna", n - 1), ("xnb", n - 1)] * old + [("hsq", n)] * now
           + [("ksum", m)] * nxt,
        6: [("lg", n - 1)] * old + [("kq", m)] * nxt,
        7: [("qTa", n + 1), ("qTb", n + 1)] * nxt + [("hout", n)] * now,
        8: [("kTa", m), ("kTb", m)] * nxt,
    }[h]


NO_BANK = ("xnorm", "qsum", "hsq", "ksum", "kq", "hout")


def build(nc, T, O):
    ctx = ExitStack()
    with ctx:
        def sb(name, shape, dt=F32):
            return ctx.enter_context(nc.sbuf_tensor(name, shape, dt))

        def sem(name):
            return ctx.enter_context(nc.semaphore(name))

        z_dram = nc.dram_tensor("z_rows", (ROWS, ZW), F32, kind="Internal").ap()
        xn_dram = nc.dram_tensor("xn_rows", (ROWS, D), F32, kind="Internal").ap()
        slot_dram = nc.dram_tensor("slot_records", (NSLOT, 4), F32, kind="Internal").ap()

        psum = ctx.enter_context(nc.psum_tensor("psum", [P, 8 * BANK], F32))

        def bank(b, n=1):
            return psum[:, b * BANK:(b + n) * BANK]

        ident = sb("ident", [P, P])
        ones = sb("ones", [P, P])
        before = sb("before", [P, P])
        route_rows = sb("route_rows", [P, 5 * NE + 5 * NT])
        logits = sb("logits", [P, NT, NG + NE])
        slot_rec = sb("slot_rec", [P, NBLK, 4])
        slot_tok = sb("slot_tok", [P, NBLK], U32)
        slot_out = sb("slot_out", [P, NBLK], U32)
        now_tok = [sb(f"now_tok{i}", [P, 1], U32) for i in range(2)]
        now_out = [sb(f"now_out{i}", [P, 1], U32) for i in range(2)]
        over_e = sb("over_e", [1, MAX_OVER + 1], I32)
        small = sb("small", [P, 512])
        arena = sb("arena", [P, 51400])

        class Area:
            def __init__(self, at=0):
                self.at = at

            def __call__(self, *shape, parts=P):
                n = int(np.prod(shape))
                a = arena[0:parts, self.at:self.at + n]
                self.at += n + n % 2
                assert self.at <= 51400, self.at
                if len(shape) == 2:
                    a = a.rearrange("p (a b) -> p a b", b=shape[1])
                if len(shape) == 3:
                    a = a.rearrange("p (a b c) -> p a b c", b=shape[1], c=shape[2])
                return a

        A = Area()
        KT = A(HA, SLOTS * P, parts=QK)
        V = A(SLOTS, HA * VD)
        Vmeta = A(HA * VD, parts=META)
        w_ukv = A(2 * HA * VD)
        cn = [A(KL + ROPE) for _ in range(2)]
        ckvT = A(P)
        kk = [A(HA, QK) for _ in range(2)]
        sqk = A(HA * NOPE)
        kjunk = A(KL)
        gat = A(NT, 2 * HM)
        GQ = A(ROWS)
        rope = A(NT, 2, ROPE)
        NM = arena[QK:QK + HM, 0:ROWS]
        pick = arena[QK:QK + HM, ROWS:ROWS + HM * P].rearrange("p (a b) -> p a b", b=P)
        dec4 = arena[QK:QK + HM, ROWS + HM * P:ROWS + HM * P + NCH]
        shared = A.at
        A = Area(shared)
        w_in = A(KD, ZW)
        xin = [A(D) for _ in range(2)]
        xT = [A(KD, P) for _ in range(2)]
        zst = [A(ZW) for _ in range(2)]
        junk = A(D)
        A = Area(shared + 8192)
        gate_rows = A(4, ROWS, parts=HM)
        gI, gF, gA, gB, gM = [A(ROWS, parts=HM) for _ in range(5)]
        A = Area(shared)
        w_out = A(KD, D)
        after_w_out = A.at
        w_uq = A(2, HA * QK)
        w_route = A(KD, NG + NE)
        z_lat = A(Z_MQ)
        z_rec = A(ZW - Z_MQ)
        cqT = A(2, P)
        qk = A(HA, QK)
        sqq = A(HA, QK)
        qT = [A(HA, P, parts=QK) for _ in range(2)]
        probs = A(NT * P)
        pT = A(NT, P)
        mix = A(D)
        mixT = A(KD, P)
        xnT = mixT
        gt = A(P)
        Dm = A(HM, P)
        chunk_mask = A(P)
        qb, kb = A(HM, P), A(HM, P)
        kw = kb
        qbT, kbT = A(HM, P), A(HM, P)
        vaug = A(HM, CAUG)
        state = [A(HM, CAUG) for _ in range(2)]
        num = A(HM, CAUG)
        og = A(HM * DV)
        hm = A(HM, DV)
        g_mh = A(HM * DV)
        g_ffn = A(D)
        g_ckv = A(KL)
        xres = A(D)
        xn = A(D)
        A = Area(0)
        rt = {k: A(*s) for k, s in {
            "el": (NT, NE), "t": (NT, NE), "oh1": (NT, NE), "oh2": (NT, NE), "m": (NT, NE), "mp": (NT + 1, NE),
            "gt": (NT, NG), "goh": (NT, NG), "ge": (NT, NG), "pos": (NT, NE), "far": (NT, NE), "rank": (NT, NE),
            "cnt": (NE,), "ov": (NE,), "ovend": (NE,), "base": (NE,), "cmp": (MAX_OVER, NE), "cols": (16, NT),
            "rec": (NT * 2, 4), "over": (MAX_OVER + 1,)}.items()}
        rt_dest = A(2, NT).bitcast(U32)
        A = Area(0)
        w1s = [A(KD, FF) for _ in range(2)]
        w3s = [A(KD, FF) for _ in range(2)]
        w2s = [A(KF, D) for _ in range(2)]
        xe = [A(D) for _ in range(2)]
        xeT = [A(KD, P) for _ in range(2)]
        th = A(FF)
        uu = A(FF)
        hh = A(FF)
        hT = A(KF, P)
        ye = [A(D) for _ in range(2)]
        sp = [0]

        def tiny(n, parts=P):
            a = small[0:parts, sp[0]:sp[0] + n]
            sp[0] += n
            assert sp[0] <= 512
            return a
        xss = [tiny(1) for _ in range(2)]
        xrs = [tiny(1) for _ in range(2)]
        g_attn = tiny(KD)
        g_cq = tiny(2)
        g_qk = tiny(3, QK)
        b_gate = tiny(2, HM)
        mstate = tiny(1, HM)
        half = tiny(16)
        eps = tiny(1)
        st_in = tiny(2)
        rs_in = tiny(2)
        krss = [tiny(1) for _ in range(2)]
        st_qk = [tiny(16) for _ in range(2)]
        rs_qk = [tiny(16) for _ in range(2)]
        nmax = tiny(HA)
        rsum = tiny(HA)
        rinv = tiny(HA)
        ropet = tiny(2 * ROPE)
        den = tiny(2 * HM)
        st_m = tiny(HM)
        rs_m = tiny(HM)
        st_x = tiny(1)
        rs_x = tiny(1)
        m_out = tiny(NCH, HM)
        m_prev = tiny(NCH, HM)
        m_last = tiny(NCH, HM)
        b_last = tiny(NCH, HM)
        decb = tiny(HM * NCH)
        b_route = tiny(NG + NE)

        fills, ring_used = pe_fills()
        RB = [3, 5, 6, 7]
        full = [sem(f"ring{i}_full") for i in range(4)]
        read = [sem(f"ring{i}_read") for i in range(4)]
        s_full, s_read = sem("scores_full"), sem("scores_read")
        pv_done, o_read = sem("values_summed"), sem("att_read")
        xt_full = [sem(f"xT{i}_full") for i in range(2)]
        xt_read = [sem(f"xT{i}_read") for i in range(2)]
        z_full = [sem(f"z{i}_full") for i in range(4)]
        z_read = [sem(f"z{i}_read") for i in range(4)]
        x_in = [sem(f"x{i}_in") for i in range(2)]
        rs_mid = [sem(f"x{i}_mean") for i in range(2)]
        zst_out = [sem(f"z_store{i}") for i in range(2)]
        x_ssq = [sem(f"x{i}_ssq") for i in range(2)]
        x_rstd = [sem(f"x{i}_rstd") for i in range(2)]
        kvw_in, const_in, win_in = sem("w_ukv_in"), sem("const_in"), sem("w_in_in")
        cache_in = [sem(f"cache{i}_in") for i in range(2)]
        gate_in, mixw_in, wout_in = sem("gate_rows_in"), sem("mix_weights_in"), sem("w_out_in")
        zl_in, zr_in = sem("z_latents_in"), sem("z_mlstm_in")
        xres_in = sem("xres_in")
        kv_out = [sem(f"kv_store{i}") for i in range(2)]
        x1_out, xn_out = sem("x1_store"), sem("xn_store")
        state_out, m_store = sem("state_store"), sem("m_store")
        vmeta_in = sem("vmeta_in")
        slots_clear = sem("slots_clear")
        half_ok = sem("half_ready")
        ones_ok = sem("ones_ready")
        kr_ssq = sem("kr_squares")
        kn_sq = sem("kn_squares")
        kv_stats = sem("qk_sums_ready")
        kv_rstd = sem("qk_rstd_ready")
        cn_ok = sem("ckv_kr_ready")
        in_ssq = sem("cq_ckv_sums")
        in_rstd = sem("cq_ckv_rstd")
        q_sq = sem("q_squares")
        q_ok = sem("q_ready")
        kk_ok = sem("k_ready")
        g_a, g_v, g_ok, g_qk_ok = sem("gate_logs"), sem("gate_dve"), sem("gate_exps"), sem("g_qk_ready")
        gq_zero, stq_ok, qs_ok = sem("gate_rows_zeroed"), sem("sums_preset"), sem("q_sums_ready")
        zero_ok = sem("mlstm_zeroed")
        packed = sem("mlstm_packed")
        d_ok, e_ok, kw_ok = sem("decay_logs"), sem("decay_exps"), sem("kw_ready")
        st1_ok = sem("state_mid")
        og_ok = sem("ogate_tanh")
        h_ok, hsq_ok, hs_ok, hr_ok = sem("h_ready"), sem("h_squares"), sem("h_sums"), sem("h_rstd")
        mm_ok = sem("mix_mlstm")
        max_ok = sem("scores_max")
        x1_sq, x1_rs, xn_ok = sem("res_squares"), sem("res_rstd"), sem("xn_ready")
        dve_link, act_link, pool_link = sem("dve_link"), sem("act_link"), sem("pool_link")
        r_dve, r_act, r_pe = sem("route_dve"), sem("route_act"), sem("route_pe")
        rec_ok, rec_out, rec_in = sem("records_ready"), sem("records_stored"), sem("records_in")
        index_steps = sem("index_steps")
        tab_ok, gather_idx, scatter_idx = sem("slot_tables_ready"), sem("gather_indices"), sem("scatter_indices")
        w_in_s = [sem(f"expert_w{i}_in") for i in range(2)]
        xe_in = [sem(f"xe{i}_in") for i in range(2)]
        xeT_full, xeT_read = sem("xeT_full"), sem("xeT_read")
        h1_full, h3_full = sem("h1_full"), sem("h3_full")
        tanh_ok, hh_ok = sem("silu_tanh"), sem("hh_ready")
        u_ok = sem("silu_ready")
        hT_full, hT_read = sem("hT_full"), sem("hT_read")
        y_full, y_read = sem("y_full"), sem("y_read")
        ye_out = [sem(f"ye{i}_store") for i in range(2)]
        ov_w, ov_xe, ov_ye = sem("over_w_in"), sem("over_xe_in"), sem("over_ye_store")

        block = ctx.enter_context(nc.Block())

        def wait_full(eng, key):
            b, k = fills[key]
            eng.wait_ge(full[b], k + 1)
            return bank(RB[b])

        def wait_read(eng, key):
            b, k = fills[key]
            eng.wait_ge(read[b], k + 1)

        def done_read(ins, key):
            ins.then_inc(read[fills[key][0]], 1)

        def chain(eng, s):
            n = [0]

            def link(ins):
                n[0] += 1
                ins.then_inc(s, 1)
                eng.wait_ge(s, n[0])
            return link

        def bc(ap, shape):
            return ap.unsqueeze(len(ap.shape)).to_broadcast(shape)

        def bc1(ap, shape):
            return ap.unsqueeze(1).to_broadcast(shape)

        def slot_of(m):
            return m + 2 if m < NC else m - NC

        def load_cache(eng, c):
            r = slice(c * P, (c + 1) * P)
            if c >= 2:
                eng.wait_ge(kk_ok, c - 1)
                b, k = fills[("ckvT", c - 2)]
                eng.wait_ge(full[b], k + 1)
                eng.wait_ge(kr_ssq, c - 1)
            eng.dma_start(cn[c % 2][:, 0:KL], T["cache_ckv"][r, :]).then_inc(cache_in[c % 2], 16)
            eng.dma_start(cn[c % 2][:, KL:], T["cache_kr"][r, :]).then_inc(cache_in[c % 2], 16)

        def ahead(eng, value):
            return value if isinstance(value, int) else eng.snap(value)

        def load_x(eng, n, s, j):
            row = ahead(eng, n * P)
            eng.wait_ge(xt_full[s], j + 1)
            eng.wait_ge(x_ssq[s], j + 1)
            eng.dma_start(xin[s], T["x_rows"][bass.ds(row, P), :]).then_inc(x_in[s], 16)

        def store_z(eng, n, s):
            row, count = ahead(eng, n * P), ahead(eng, n + 1)
            for c in range(4):
                eng.wait_ge(z_read[c], count)
            eng.dma_start(z_dram[bass.ds(row, P), :], zst[s]).then_inc(zst_out[s], 16)

        def load_expert(eng, e, s, signal, freed=None, count=None):
            row_up, row_down = ahead(eng, e * D), ahead(eng, e * FF)
            if freed is not None:
                eng.wait_ge(freed, ahead(eng, count))
            load_part(eng, row_up, w1s[s], "w1", signal)
            load_part(eng, row_up, w3s[s], "w3", signal)
            load_part(eng, row_down, w2s[s], "w2", signal)

        def load_part(eng, row, dst, src, signal):
            rows = T[src].rearrange("e a n -> (e a) n")[bass.ds(row, T[src].shape[1]), :]
            eng.dma_start(dst, rows.rearrange("(k p) n -> p k n", p=P)).then_inc(signal, 16)

        def gate_col(b):
            return slot_rec[:, bass.ds(b, 1), 2:3].rearrange("p a b -> p (a b)")

        def take_pT(copy, o, part, at, q, key):
            whole = [p for p in part if p[3] == P]
            ins = None
            if whole:
                k = len(whole)
                src = o[:, 0:k * P].rearrange("p (a b) -> p a b", b=P)
                ins = copy(pT[:, at:at + k, 0:q], src[:, :, 0:q])
            if len(whole) < len(part):
                k, w = len(whole), part[-1][3]
                ins = copy(pT[0:w, at + k, 0:q], o[0:w, k * P:k * P + q])
            done_read(ins, key)

        def wait_values(eng, n, h):
            if (n, h) != (0, 0):
                eng.wait_ge(pv_done, n * HA + h)

        @block.sync
        def _(sp_):
            sp_.dma_start(ident[:], T["ident"]).then_inc(const_in, 16)
            sp_.dma_start(w_ukv, T["w_ukv"]).then_inc(kvw_in, 16)
            for c in range(2):
                load_cache(sp_, c)
            sp_.dma_start(g_attn, T["g_attn"]).then_inc(const_in, 16)
            sp_.dma_start(xin[0], T["x_rows"][0:P, :]).then_inc(x_in[0], 16)
            sp_.dma_start(w_in, T["w_in"].rearrange("(k p) n -> p k n", p=P)).then_inc(win_in, 16)
            sp_.dma_start(xin[1], T["x_rows"][P:2 * P, :]).then_inc(x_in[1], 16)
            sp_.dma_start(slot_dram, T["empty_slots"]).then_inc(slots_clear, 16)
            sp_.dma_start(before[:], T["before"]).then_inc(mixw_in, 16)
            sp_.dma_start(route_rows[:], T["route_rows"]).then_inc(mixw_in, 16)
            for dst, src in ((g_cq, "g_cq"), (g_qk[:, 0:1], "g_q"), (g_qk[:, 1:2], "g_k"), (b_gate, "b_gate"),
                             (mstate, "state_m")):
                sp_.dma_start(dst, T[src]).then_inc(mixw_in, 16)
            sp_.dma_start(b_route, T["b_route"].to_broadcast([P, NG + NE])).then_inc(mixw_in, 16)
            sp_.dma_start(rope, T["rope"].rearrange("p (n a r) -> p n a r", n=NT, a=2)).then_inc(mixw_in, 16)
            sp_.dma_start(pick, T["pick_head"].rearrange("p (a b) -> p a b", b=P)).then_inc(mixw_in, 16)
            for c in range(2, NC):
                load_cache(sp_, c)
            with sp_.Fori(0, NT // 2 - 1) as j:
                for s in range(2):
                    load_x(sp_, 2 * j + s + 2, s, j)
                    store_z(sp_, 2 * j + s, s)
            load_x(sp_, NT - 1, 0, NT // 2 - 1)
            for n in range(NT - 3, NT):
                store_z(sp_, n, n % 2)
            for s in range(2):
                sp_.wait_ge(zst_out[s], 16 * (NT // 2 + (s == 0)))
            for i in range(4):
                sp_.wait_ge(z_full[i], NT)
            sp_.dma_start(gate_rows, T["gate_rows"].rearrange("p (a b) -> p a b", b=ROWS)).then_inc(gate_in, 16)
            sp_.dma_start(w_out, T["w_out"].rearrange("(k p) n -> p k n", p=P)).then_inc(wout_in, 16)
            sp_.wait_ge(g_ok, 4)
            sp_.dma_start(z_lat, z_dram[0:P, 0:Z_MQ]).then_inc(zl_in, 16)
            sp_.dma_start(z_rec, z_dram[0:P, Z_MQ:]).then_inc(zr_in, 16)
            sp_.dma_start(w_uq, T["w_uq"].rearrange("(k p) n -> p k n", p=P)).then_inc(wout_in, 16)
            sp_.dma_start(w_route, T["w_route"].rearrange("(k p) n -> p k n", p=P)).then_inc(wout_in, 16)
            sp_.dma_start(chunk_mask, T["chunk_mask"]).then_inc(wout_in, 16)
            sp_.dma_start(g_mh, T["g_mh"].to_broadcast([P, HM * DV])).then_inc(wout_in, 16)
            sp_.dma_start(g_ffn, T["g_ffn"].to_broadcast([P, D])).then_inc(wout_in, 16)
            sp_.dma_start(g_ckv, T["g_ckv"].to_broadcast([P, KL])).then_inc(wout_in, 16)
            sp_.wait_ge(zero_ok, 5)
            sp_.dma_start(state[0][0:DK], T["state_c"].rearrange("p (a b) -> p a b", b=CAUG)).then_inc(wout_in, 16)
            for col, c in ((0, NCH - 1), (1, 0)):
                sp_.dma_start(O["m_both"][col], m_out[:, c:c + 1]).then_inc(m_store, 16)
            for n in range(-1, NT + 1):
                if n >= 1:
                    if n >= 2:
                        sp_.wait_ge(x1_out, 16 * (n - 1))
                        sp_.wait_ge(xn_ok, n - 1)
                    sp_.dma_start(xres, T["x_rows"][(n - 1) * P:n * P, :]).then_inc(xres_in, 16)
                if n + 1 < NT:
                    r = slice((n + 1) * P, (n + 2) * P)
                    src = cn[(NC + n + 1) % 2]
                    sp_.wait_ge(cn_ok, n + 2)
                    sp_.dma_start(O["ckv"][r, :], src[:, 0:KL]).then_inc(kv_out[(n + 1) % 2], 16)
                    sp_.dma_start(O["krope"][r, :], src[:, KL:]).then_inc(kv_out[(n + 1) % 2], 16)
                if n + 2 < NT:
                    sp_.wait_ge(in_ssq, 2 * (n + 2))
                    wait_full(sp_, ("cqT", n + 1))
                    sp_.dma_start(z_lat, z_dram[(n + 2) * P:(n + 3) * P, 0:Z_MQ]).then_inc(zl_in, 16)
                if n == -1:
                    wait_read(sp_, ("v", NC))
                    sp_.dma_start(Vmeta, V[DEC:DEC + META, 0, :]).then_inc(vmeta_in, 16)
                if n == 0:
                    sp_.wait_ge(st1_ok, HM)
                    sp_.dma_start(O["c_sample"], state[1][DK:P].rearrange("p a b -> p (a b)")).then_inc(state_out, 16)
                if n >= 1:
                    r = slice((n - 1) * P, n * P)
                    wait_read(sp_, ("o1", n - 1))
                    sp_.dma_start(O["y"][r, :], xres).then_inc(x1_out, 16)
                    sp_.wait_ge(xn_ok, n)
                    sp_.dma_start(xn_dram[r, :], xn).then_inc(xn_out, 16)
                if 0 <= n and n + 1 < NT:
                    sp_.wait_ge(packed, 5 * (n + 1))
                    sp_.wait_ge(og_ok, n + 1)
                    sp_.dma_start(z_rec, z_dram[(n + 1) * P:(n + 2) * P, Z_MQ:]).then_inc(zr_in, 16)
            wait_read(sp_, ("ub", NT - 1))
            sp_.dma_start(O["c_prompt"], state[NT % 2][0:DK].rearrange("p a b -> p (a b)")).then_inc(state_out, 16)
            sp_.wait_ge(state_out, 32)
            sp_.wait_ge(m_store, 32)
            sp_.wait_ge(kv_out[0], 32 * ((NT + 1) // 2))
            sp_.wait_ge(kv_out[1], 32 * (NT // 2))
            sp_.wait_ge(x1_out, 16 * NT)
            sp_.wait_ge(xn_out, 16 * NT)
            wait_read(sp_, ("lg", NT - 1))
            load_expert(sp_, 1, 1, w_in_s[1])
            load_part(sp_, 0, w3s[0], "w3", w_in_s[0])
            load_part(sp_, 0, w2s[0], "w2", w_in_s[0])
            sp_.wait_ge(rec_out, 16 * 2 * NT)
            sp_.dma_start(slot_rec[:], slot_dram.rearrange("(b p) c -> p b c", p=P)).then_inc(rec_in, 16)
            sp_.wait_ge(tab_ok, 1)
            load_part(sp_, 0, w1s[0], "w1", w_in_s[0])
            with sp_.Fori(0, NE // 2 - 1) as j:
                for s in range(2):
                    load_expert(sp_, 2 * j + s + 2, s, w_in_s[s], y_full, 2 * j + s + 1)
            sp_.wait_ge(y_full, NE)
            total = sp_.value_load(over_e[0:1, MAX_OVER:MAX_OVER + 1], min_val=0, max_val=MAX_OVER)
            with sp_.Fori(0, MAX_OVER) as j:
                with sp_.If(j < total):
                    e = sp_.value_load(over_e[0:1, bass.ds(j, 1)], min_val=0, max_val=NE - 1)
                    load_expert(sp_, e, 0, ov_w, y_full, NE + j)
        @block.tensor
        def _(pe):
            order = sorted(fills, key=lambda k: (fills[k][1] * 4 + fills[k][0]))
            at = [0]

            def open_bank(key):
                assert order[at[0]] == key, (order[at[0]], key)
                at[0] += 1
                b, k = fills[key]
                if k:
                    pe.wait_ge(read[b], k)
                return bank(RB[b])

            def filled(ins, key):
                ins.then_inc(full[fills[key][0]], 1)

            def transposes(key, parts, width, sources):
                o = open_bank(key)
                for i, src in enumerate(sources):
                    rows = src.shape[0]
                    ins = pe.transpose(o[0:width, i * P:i * P + rows], src, ident[0:rows, 0:rows])
                filled(ins, key)

            def key_values(m, what):
                if what == "ckvT":
                    if m < NC:
                        pe.wait_ge(cache_in[m % 2], 32 * (m // 2 + 1))
                    else:
                        pe.wait_ge(cn_ok, m - NC + 1)
                    transposes(("ckvT", m), P, KL, [cn[m % 2][:, 0:KL]])
                if what in ("kn", "v"):
                    wait_read(pe, ("ckvT", m))
                    off = 0 if what == "kn" else HA * NOPE
                    o = open_bank((what, m))
                    filled(pe.matmul(o, ckvT, w_ukv[:, off:off + BANK], start=True, stop=True), (what, m))
                if what in ("kTa", "kTb"):
                    pe.wait_ge(kk_ok, m + 1)
                    h0 = 0 if what == "kTa" else 4
                    transposes((what, m), P, QK, [kk[m % 2][:, h, :] for h in range(h0, h0 + 4)])

            pe.wait_ge(const_in, 16)
            pe.wait_ge(kvw_in, 16)
            for c in range(NC + 1):
                if c < NC:
                    for what in ("ckvT", "kn", "v"):
                        key_values(c, what)
                if c >= 1:
                    key_values(c - 1, "kTa")
                    key_values(c - 1, "kTb")
            for b in range(4):
                pe.wait_ge(read[b], [sum(1 for k in order[:at[0]] if fills[k][0] == i) for i in range(4)][b])

            def x_transposes(s, j):
                pe.wait_ge(x_in[s], 16 * (j + 1))
                pe.wait_ge(xt_read[s], j)
                o = bank(2 * s, 2)
                for k in range(KD):
                    ins = pe.transpose(o[:, k * P:(k + 1) * P], xin[s][:, k * P:(k + 1) * P], ident[:])
                ins.then_inc(xt_full[s], 1)

            def x_gemm(s, n, j):
                pe.wait_ge(xt_read[s], j + 1)
                for c, (lo, hi) in enumerate(Z_CHUNKS):
                    pe.wait_ge(z_read[c], n)
                    o = bank(4 + c)
                    for k in range(KD):
                        ins = pe.matmul(o[:, 0:hi - lo], xT[s][:, k, :], w_in[:, k, lo:hi],
                                        start=(k == 0), stop=(k == KD - 1))
                    ins.then_inc(z_full[c], 1)

            x_transposes(0, 0)
            pe.wait_ge(win_in, 16)
            with pe.Fori(0, NT // 2) as j:
                x_transposes(1, j)
                x_gemm(0, 2 * j, j)
                x_transposes(0, j + 1)
                x_gemm(1, 2 * j + 1, j)
            x_gemm(0, NT - 1, NT // 2)
            for c in range(4):
                pe.wait_ge(z_read[c], NT)

            for g in range(2):
                if g:
                    pe.wait_ge(s_read, 1)
                o = bank(0, 3)
                for n in range(NT):
                    ins = pe.transpose(o[0:HM, n * P:(n + 1) * P], gat[:, n, g * HM:(g + 1) * HM], ident[:])
                ins.then_inc(s_full, 1)
            pe.wait_ge(g_ok, 4)
            pe.wait_ge(mixw_in, 16 * 10)
            pe.wait_ge(s_read, 2)
            for h in range(HM):
                ins = pe.matmul(bank(0)[:, h * NCH:(h + 1) * NCH], pick[:, h, :], dec4, start=True, stop=True)
            ins.then_inc(s_full, 1)

            def step(key):
                what, n = key
                if what in NO_BANK:
                    return
                if what in ("ckvT", "kn", "v", "kTa", "kTb"):
                    key_values(n, what)
                elif what == "cqT":
                    pe.wait_ge(zl_in, 16 * (n + 1))
                    transposes(key, P, P, [z_lat[:, Z_CQ + i * P:Z_CQ + (i + 1) * P] for i in range(2)])
                elif what in ("q0", "q1"):
                    wait_read(pe, ("cqT", n))
                    o = open_bank(key)
                    w = HA * QK // 2
                    lo = 0 if what == "q0" else w
                    for k in range(2):
                        ins = pe.matmul(o[:, 0:w], cqT[:, k, :], w_uq[:, k, lo:lo + w], start=(k == 0), stop=(k == 1))
                    filled(ins, key)
                elif what in ("qTa", "qTb"):
                    pe.wait_ge(q_ok, n + 1)
                    h0 = 0 if what == "qTa" else 4
                    transposes(key, P, QK, [qk[:, h, :] for h in range(h0, h0 + 4)])
                elif what == "gt":
                    transposes(key, P, P, [GQ[:, n * P:(n + 1) * P]])
                elif what == "nm":
                    o = open_bank(key)
                    for h in range(HM):
                        ins = pe.matmul(o[:, h * P:(h + 1) * P], pick[:, h, :], NM[:, n * P:(n + 1) * P],
                                        start=True, stop=True)
                    filled(ins, key)
                elif what in ("qbT", "kbT"):
                    pe.wait_ge(packed, 5 * (n + 1))
                    src = qb if what == "qbT" else kb
                    transposes(key, P, P, [src[:, h, :] for h in range(HM)])
                elif what == "qkm":
                    wait_read(pe, ("qbT", n))
                    wait_read(pe, ("kbT", n))
                    o = open_bank(key)
                    for h in range(HM):
                        ins = pe.matmul(o[:, h * P:(h + 1) * P], kbT[:, h, :], qbT[:, h, :], start=True, stop=True)
                    filled(ins, key)
                elif what in ("ua", "ub", "ia", "ib", "na", "nb"):
                    lhs, rhs = {"u": (kw, vaug), "i": (qbT, state[n % 2]), "n": (Dm, vaug)}[what[0]]
                    if what == "ua":
                        pe.wait_ge(kw_ok, n + 1)
                    if what == "ia":
                        pe.wait_ge(st1_ok, 4 * (n + 1))
                        if n:
                            wait_read(pe, ("ub", n - 1))
                    if what == "na":
                        wait_read(pe, ("qkm", n))
                    o = open_bank(key)
                    h0 = 0 if what[1] == "a" else 2
                    for h in range(h0, h0 + 2):
                        ins = pe.matmul(o[:, (h - h0) * CAUG:(h - h0 + 1) * CAUG], lhs[:, h, :], rhs[:, h, :],
                                        start=True, stop=True)
                    filled(ins, key)
                elif what in ("mxa", "mxb"):
                    pe.wait_ge(mm_ok, n + 1)
                    pe.wait_ge(o_read, n + 1)
                    k0 = 0 if what == "mxa" else 4
                    transposes(key, P, P, [mix[:, k * P:(k + 1) * P] for k in range(k0, k0 + 4)])
                elif what in ("o0", "o1"):
                    wait_read(pe, ("mxa", n))
                    wait_read(pe, ("mxb", n))
                    o = open_bank(key)
                    lo = 0 if what == "o0" else BANK
                    for k in range(KD):
                        ins = pe.matmul(o, mixT[:, k, :], w_out[:, k, lo:lo + BANK], start=(k == 0), stop=(k == KD - 1))
                    filled(ins, key)
                elif what in ("xna", "xnb"):
                    pe.wait_ge(xn_ok, n + 1)
                    k0 = 0 if what == "xna" else 4
                    transposes(key, P, P, [xn[:, k * P:(k + 1) * P] for k in range(k0, k0 + 4)])
                elif what == "lg":
                    wait_read(pe, ("xna", n))
                    wait_read(pe, ("xnb", n))
                    o = open_bank(key)
                    for k in range(KD):
                        ins = pe.matmul(o[:, 0:NG + NE], xnT[:, k, :], w_route[:, k, :], start=(k == 0), stop=(k == KD - 1))
                    filled(ins, key)
                else:
                    raise AssertionError(what)

            def scores(n, h):
                pe.wait_ge(s_read, 3 + n * HA + h)
                if h == 0:
                    wait_read(pe, ("qTa", n))
                    wait_read(pe, ("kTa", NC + n))
                    wait_read(pe, ("kTb", NC + n))
                if h == 4:
                    wait_read(pe, ("qTb", n))
                q = DEC if n == 0 else P
                blocks = key_blocks(n)
                o = bank(0, 3)
                last = blocks[-1]
                runs = [(i, min(i + BANK, last[0])) for i in range(0, last[0], BANK)]
                for lo, hi in runs:
                    k0 = blocks[0][1] * P + lo
                    pe.matmul(o[0:q, lo:hi], qT[n % 2][:, h, 0:q], KT[:, h, k0:k0 + hi - lo], start=True, stop=True)
                lo, _, k0, w = last
                pe.matmul(o[0:q, lo:lo + w], qT[n % 2][:, h, 0:q], KT[:, h, k0:k0 + w],
                          start=True, stop=True).then_inc(s_full, 1)

            def probs_transposes(n, h):
                pe.wait_ge(s_read, 3 + n * HA + h + 1)
                q = DEC if n == 0 else P
                blocks = key_blocks(n)
                for g in range((len(blocks) + 3) // 4):
                    key = ("pT", n, h, g)
                    o = open_bank(key)
                    for i, (lo, _, _, w) in enumerate(blocks[4 * g:4 * g + 4]):
                        ins = pe.transpose(o[0:w, i * P:i * P + q], probs[0:q, lo:lo + w], ident[0:q, 0:q])
                    filled(ins, key)

            def values(n, h):
                q = DEC if n == 0 else P
                blocks = key_blocks(n)
                for g in range((len(blocks) + 3) // 4):
                    wait_read(pe, ("pT", n, h, g))
                if h == 0:
                    wait_read(pe, ("v", NC + n))
                    pe.wait_ge(vmeta_in, 16)
                    if n:
                        pe.wait_ge(o_read, n)
                o = bank(4)[0:q, h * VD:(h + 1) * VD]
                for i, (_, slot, k0, w) in enumerate(blocks):
                    v = Vmeta[:, h * VD:(h + 1) * VD] if k0 else V[0:w, slot, h * VD:(h + 1) * VD]
                    ins = pe.matmul(o, pT[0:w, i, 0:q], v, start=(i == 0), stop=(i == len(blocks) - 1))
                ins.then_inc(pv_done, 1)

            pe.wait_ge(wout_in, 16 * 8)
            pe.wait_ge(s_read, 3)
            for n in range(-1, NT + 1):
                now = 0 <= n < NT
                if now:
                    scores(n, 0)
                for h in range(HA):
                    for key in filler(n, h):
                        step(key)
                    if now:
                        if h:
                            values(n, h - 1)
                        probs_transposes(n, h)
                        if h + 1 < HA:
                            scores(n, h + 1)
                for key in filler(n, HA):
                    step(key)
                if now:
                    values(n, HA - 1)
            assert at[0] == len(order)

            for b in range(4):
                pe.wait_ge(read[b], ring_used[b])
            pe.wait_ge(r_dve, 1)
            pe.wait_ge(ones_ok, 1)
            w = NT * NE
            pe.matmul(bank(0)[:, 0:w], before[:], rt["m"].rearrange("p a b -> p (a b)"), start=True, stop=False)
            pe.matmul(bank(0)[:, 0:w], ones[:], rt["mp"][:, 0:NT].rearrange("p a b -> p (a b)"), start=False, stop=True)
            pe.matmul(bank(1)[:, 0:NE], ones[:], rt["mp"][:, NT], start=True, stop=True).then_inc(r_pe, 1)
            pe.wait_ge(tab_ok, 1)

            def gather_transposes(s, b, arrived, count):
                pe.wait_ge(arrived, count)
                pe.wait_ge(xeT_read, b)
                for k in range(KD):
                    ins = pe.transpose(bank(0, 2)[:, k * P:(k + 1) * P], xe[s][:, k * P:(k + 1) * P], ident[:])
                ins.then_inc(xeT_full, 1)

            def up(s, b, arrived, count):
                pe.wait_ge(arrived, count)
                pe.wait_ge(xeT_read, b + 1)
                pe.wait_ge(hh_ok, b)
                for w, o, signal in ((w1s[s], 2, h1_full), (w3s[s], 3, h3_full)):
                    for k in range(KD):
                        ins = pe.matmul(bank(o), xeT[s][:, k, :], w[:, k, :], start=(k == 0), stop=(k == KD - 1))
                    ins.then_inc(signal, 1)

            def down(s, b):
                pe.wait_ge(hh_ok, b + 1)
                pe.wait_ge(hT_read, b)
                for k in range(KF):
                    ins = pe.transpose(bank(4)[:, k * P:(k + 1) * P], hh[:, k * P:(k + 1) * P], ident[:])
                ins.then_inc(hT_full, 1)
                pe.wait_ge(hT_read, b + 1)
                pe.wait_ge(y_read, b)
                for c in range(2):
                    for k in range(KF):
                        ins = pe.matmul(bank(5 + c), hT[:, k, :], w2s[s][:, k, c * BANK:(c + 1) * BANK],
                                        start=(k == 0), stop=(k == KF - 1))
                ins.then_inc(y_full, 1)

            gather_transposes(0, 0, xe_in[0], 16)
            with pe.Fori(0, NE // 2 - 1) as j:
                for s in range(2):
                    up(s, 2 * j + s, w_in_s[s], 48 * j + 48)
                    gather_transposes(1 - s, 2 * j + s + 1, xe_in[1 - s], 16 * j + 16 * (1 + s))
                    down(s, 2 * j + s)
            up(0, NE - 2, w_in_s[0], 48 * (NE // 2))
            gather_transposes(1, NE - 1, xe_in[1], 16 * (NE // 2))
            down(0, NE - 2)
            up(1, NE - 1, w_in_s[1], 48 * (NE // 2))
            down(1, NE - 1)
            total = pe.value_load(over_e[0:1, MAX_OVER:MAX_OVER + 1], min_val=0, max_val=MAX_OVER)
            with pe.Fori(0, MAX_OVER) as j:
                with pe.If(j < total):
                    gather_transposes(0, NE + j, ov_xe, 16 * j + 16)
                    up(0, NE + j, ov_w, 48 * j + 48)
                    down(0, NE + j)

        @block.scalar
        def _(act):
            link = chain(act, act_link)

            def kv_squares(m):
                if m < NC:
                    act.wait_ge(cache_in[m % 2], 32 * (m // 2 + 1))
                else:
                    act.wait_ge(cn_ok, m - NC + 1)
                if m >= 2:
                    act.wait_ge(kv_stats, m - 1)
                act.wait_ge(kr_ssq, m)
                if m > NC:
                    act.wait_ge(in_ssq, 2 * (m - NC + 1))
                act.activation(kjunk[:, 0:ROPE], cn[m % 2][:, KL:], ACT.Square, accum_out=krss[m % 2]).then_inc(kr_ssq, 1)

            def kv_latent(m):
                o = wait_full(act, ("ckvT", m))
                if m:
                    wait_full(act, ("v", m - 1))
                done_read(act.activation(ckvT, o[:, 0:P], ACT.Copy), ("ckvT", m))

            def kv_products(m):
                o = wait_full(act, ("kn", m))
                if m:
                    act.wait_ge(kv_stats, m)
                act.activation(sqk, o, ACT.Square).then_inc(kn_sq, 1)
                if m >= 2:
                    wait_full(act, ("kTb", m - 2))
                done_read(act.activation(kk[m % 2][:, :, 0:NOPE], o.rearrange("p (h d) -> p h d", d=NOPE), ACT.Copy),
                          ("kn", m))
                o = wait_full(act, ("v", m))
                n = m - NC
                if n >= 2:
                    act.wait_ge(pv_done, HA)
                done_read(act.activation(V[:, slot_of(m), :], o, ACT.Copy), ("v", m))

            def kT_take(m, what):
                o = wait_full(act, (what, m))
                n = m - NC
                if n >= 2:
                    act.wait_ge(pv_done, HA)
                h0 = 0 if what == "kTa" else 4
                at = slot_of(m) * P
                done_read(act.activation(KT[:, h0:h0 + 4, at:at + P],
                                         o[0:QK].rearrange("p (a b) -> p a b", b=P), ACT.Copy), (what, m))

            for c in range(NC + 1):
                if c < NC:
                    kv_squares(c)
                    kv_latent(c)
                    kv_products(c)
                if c >= 1:
                    kT_take(c - 1, "kTa")
                    kT_take(c - 1, "kTb")

            def x_squares(s, j):
                act.wait_ge(x_in[s], 16 * (j + 1))
                act.wait_ge(x_ssq[1 - s], j + s)
                act.activation(junk, xin[s], ACT.Square, scale=1.0 / 32, accum_out=xss[s]).then_inc(x_ssq[s], 1)

            def z_take(s, n, j):
                act.wait_ge(x_rstd[s], j + 1)
                act.wait_ge(zst_out[s], 16 * j)
                for c in (0, 2):
                    lo, hi = Z_CHUNKS[c]
                    act.wait_ge(z_full[c], n + 1)
                    if c == 0:
                        act.activation(gat[:, bass.ds(n, 1), :].rearrange("p a b -> p (a b)"),
                                       bank(4)[:, Z_GATE:Z_GATE + 2 * HM], ACT.Copy, scale=xrs[s])
                    act.activation(zst[s][:, lo:hi], bank(4 + c)[:, 0:hi - lo], ACT.Copy,
                                   scale=xrs[s]).then_inc(z_read[c], 1)

            x_squares(0, 0)
            with act.Fori(0, NT // 2) as j:
                x_squares(1, j)
                z_take(0, 2 * j, j)
                x_squares(0, j + 1)
                z_take(1, 2 * j + 1, j)
            z_take(0, NT - 1, NT // 2)

            act.wait_ge(s_read, 2)
            link(act.activation(gA, gF, ACT.Abs))
            link(act.activation(gA, gA, ACT.Exp, scale=-1.0))
            act.activation(gA, gA, ACT.Ln, bias=1.0).then_inc(g_a, 1)
            act.wait_ge(g_v, 1)
            for i in range(3):
                rows = GQ[32 * (i + 1):32 * (i + 1) + HM]
                act.activation(rows, rows, ACT.Exp).then_inc(g_ok, 1)
            act.activation(dec4, dec4, ACT.Exp).then_inc(g_ok, 1)

            def fill_work(key):
                what, n = key
                if what == "cqT":
                    act.wait_ge(zl_in, 16 * (n + 1))
                    if n:
                        act.wait_ge(in_rstd, n)
                    z = z_lat
                    act.activation(sqq.rearrange("p a b -> p (a b)")[:, 0:QL], z[:, Z_CQ:Z_CQ + QL], ACT.Square,
                                   scale=QL ** -0.5, accum_out=st_in[:, 0:1]).then_inc(in_ssq, 1)
                    act.wait_ge(kr_ssq, NC + n)
                    act.activation(kjunk, z[:, Z_CKV:Z_CKV + KL], ACT.Square,
                                   scale=KL ** -0.5, accum_out=st_in[:, 1:2]).then_inc(in_ssq, 1)
                elif what == "ckvT":
                    kv_squares(n)
                    kv_latent(n)
                elif what in ("q0", "q1"):
                    w = HA * QK // 2
                    lo = 0 if what == "q0" else w
                    o = wait_full(act, key)
                    act.wait_ge(in_rstd, n + 1)
                    if n and what == "q0":
                        wait_full(act, ("qTb", n - 1))
                    dst = qk.rearrange("p a b -> p (a b)")[:, lo:lo + w]
                    done_read(act.activation(dst, o[:, 0:w], ACT.Copy, scale=rs_in[:, 0:1]), key)
                    if what == "q1":
                        wait_read(act, ("q0", n))
                        wait_read(act, ("q1", n))
                        act.activation(sqq, qk, ACT.Square).then_inc(q_sq, 1)
                elif what == "kn":
                    kv_products(n)
                elif what == "v":
                    pass
                elif what in ("kTa", "kTb"):
                    kT_take(n, what)
                elif what in ("qTa", "qTb"):
                    o = wait_full(act, key)
                    h0 = 0 if what == "qTa" else 4
                    done_read(act.activation(qT[n % 2][:, h0:h0 + 4, :], o[0:QK].rearrange("p (a b) -> p a b", b=P),
                                             ACT.Copy, scale=g_qk[:, 2:3]), key)
                elif what == "gt":
                    o = wait_full(act, key)
                    if n:
                        act.wait_ge(h_ok, n)
                        act.wait_ge(kw_ok, n)
                    done_read(act.activation(gt, o[:, 0:P], ACT.Copy), key)
                elif what == "nm":
                    act.wait_ge(zr_in, 16 * (n + 1))
                    if n:
                        act.wait_ge(mm_ok, n)
                    act.activation(og, z_rec[:, Z_MO - Z_MQ:], ACT.Tanh, scale=0.5).then_inc(og_ok, 1)
                    act.wait_ge(d_ok, n + 1)
                    act.activation(Dm, Dm, ACT.Exp).then_inc(e_ok, 1)
                elif what == "qbT":
                    o = wait_full(act, key)
                    done_read(act.activation(qbT, o.rearrange("p (a b) -> p a b", b=P), ACT.Copy), key)
                elif what == "hsq":
                    act.wait_ge(h_ok, n + 1)
                    act.activation(Dm, hm, ACT.Square).then_inc(hsq_ok, 1)
                elif what == "mxa":
                    o = wait_full(act, key)
                    if n:
                        wait_full(act, ("lg", n - 1))
                    done_read(act.activation(mixT[:, 0:4], o.rearrange("p (a b) -> p a b", b=P), ACT.Copy), key)
                elif what == "o1":
                    wait_read(act, ("o1", n))
                    if n:
                        act.wait_ge(xn_out, 16 * n)
                        wait_full(act, ("xnb", n - 1))
                    act.activation(xn, xres, ACT.Square, scale=1.0 / 32, accum_out=st_x).then_inc(x1_sq, 1)
                elif what == "xna":
                    o = wait_full(act, key)
                    wait_full(act, ("o1", n))
                    done_read(act.activation(xnT[:, 0:4], o.rearrange("p (a b) -> p a b", b=P), ACT.Copy), key)

            def exps(n, h):
                q = DEC if n == 0 else P
                last = key_blocks(n)[-1]
                w = last[0] + last[3]
                act.wait_ge(max_ok, n * HA + h + 1)
                if n or h:
                    pn, ph = (n, h - 1) if h else (n - 1, HA - 1)
                    g = (len(key_blocks(pn)) + 3) // 4 - 1
                    wait_full(act, ("pT", pn, ph, g))
                if h == 0 and n:
                    act.wait_ge(o_read, n)
                act.activation(probs[0:q, 0:w], bank(0, 3)[0:q, 0:w], ACT.Exp, bias=nmax[0:q, h:h + 1],
                               accum_out=rsum[0:q, h:h + 1]).then_inc(s_read, 1)

            def pT_take(n, h):
                q = DEC if n == 0 else P
                blocks = key_blocks(n)
                for g in range(1, (len(blocks) + 3) // 4, 2):
                    part = blocks[4 * g:4 * g + 4]
                    key = ("pT", n, h, g)
                    o = wait_full(act, key)
                    wait_values(act, n, h)
                    take_pT(lambda d, s: act.activation(d, s, ACT.Copy), o, part, 4 * g, q, key)

            act.wait_ge(wout_in, 16 * 8)
            act.wait_ge(g_qk_ok, 1)
            act.wait_ge(s_read, 3)
            act.wait_ge(mixw_in, 16 * 10)
            for n in range(-1, NT + 1):
                now = 0 <= n < NT
                if now:
                    exps(n, 0)
                for h in range(HA):
                    for key in filler(n, h):
                        fill_work(key)
                    if now:
                        pT_take(n, h)
                        if h + 1 < HA:
                            exps(n, h + 1)
                for key in filler(n, HA):
                    fill_work(key)

            act.wait_ge(r_dve, 1)
            act.activation(rt["ge"], rt["ge"], ACT.Exp).then_inc(r_act, 1)
            act.activation(rt["cols"][:, 6], rt["cols"][:, 6], ACT.Exp).then_inc(r_act, 1)

            def silu_tanh(b):
                act.wait_ge(h1_full, b + 1)
                act.wait_ge(hh_ok, b)
                act.activation(th, bank(2), ACT.Tanh, scale=0.5).then_inc(tanh_ok, 1)

            def y_take(s, b, col, out_sem, count):
                act.wait_ge(y_full, b + 1)
                act.wait_ge(out_sem, count)
                act.activation(ye[s], bank(5, 2), ACT.Copy, scale=gate_col(col)).then_inc(y_read, 1)

            act.wait_ge(tab_ok, 1)
            with act.Fori(0, NE // 2) as j:
                for s in range(2):
                    b = 2 * j + s
                    silu_tanh(b)
                    y_take(s, b, b, ye_out[s], 16 * j)
            total = act.value_load(over_e[0:1, MAX_OVER:MAX_OVER + 1], min_val=0, max_val=MAX_OVER)
            act.wait_ge(ye_out[0], 16 * (NE // 2))
            with act.Fori(0, MAX_OVER) as j:
                with act.If(j < total):
                    silu_tanh(NE + j)
                    y_take(0, NE + j, NE + j, ov_ye, 16 * j)

        @block.gpsimd
        def _(pool):
            link = chain(pool, pool_link)
            pool.memset(half, -0.5).then_inc(half_ok, 1)
            pool.wait_ge(half_ok, 1)
            pool.memset(eps, EPS).then_inc(half_ok, 1)
            pool.wait_ge(half_ok, 2)
            pool.memset(ones[:], 1.0).then_inc(ones_ok, 1)
            pool.wait_ge(ones_ok, 1)

            def rsqrt(dst, src, scale, signal, count):
                link(pool.tensor_scalar(dst, src, scale, EPS, ALU.mult, ALU.add))
                n = dst.shape[-1]
                pool.tensor_tensor(dst, dst, half[:, 0:n], ALU.pow).then_inc(signal, 1)
                pool.wait_ge(signal, count)

            def kv_rstd_of(m):
                pool.wait_ge(kv_stats, m + 1)
                rsqrt(rs_qk[m % 2], st_qk[m % 2], 1.0 / QK, kv_rstd, m + 1)

            for c in range(NC):
                kv_rstd_of(c)
            def row_rstd(s, j, before_it=None):
                pool.wait_ge(x_ssq[s], j + 1)
                if before_it is not None:
                    pool.wait_ge(z_read[2], before_it)
                    pool.wait_ge(z_read[3], before_it)
                pool.tensor_tensor(xrs[s], xss[s], eps, ALU.add).then_inc(rs_mid[s], 1)
                pool.wait_ge(rs_mid[s], j + 1)
                pool.tensor_tensor(xrs[s], xrs[s], half[:, 0:1], ALU.pow).then_inc(x_rstd[s], 1)
                pool.wait_ge(x_rstd[s], j + 1)

            row_rstd(0, 0)
            with pool.Fori(0, NT // 2) as j:
                row_rstd(1, j, 2 * j)
                row_rstd(0, j + 1, 2 * j + 1)
            pool.wait_ge(g_ok, 4)
            zero = chain(pool, zero_ok)
            for t in (qb, kb, state[0], state[1]):
                zero(pool.memset(t, 0.0))
            zero(pool.memset(vaug[:, :, DV:], 1.0))

            pack = chain(pool, packed)

            def pool_work(key):
                what, n = key
                if what == "gt":
                    pool.wait_ge(zr_in, 16 * (n + 1))
                    if n:
                        wait_full(pool, ("kbT", n - 1))
                        wait_full(pool, ("nb", n - 1))
                        pool.wait_ge(kw_ok, n)
                    for i in range(2):
                        r = slice(i * CH, (i + 1) * CH)
                        src = z_rec[r, 0:HM * DK].rearrange("p (h d) -> p h d", d=DK)
                        pack(pool.tensor_copy(qb[r, :, i * DK:(i + 1) * DK], src))
                        src = z_rec[r, Z_MK - Z_MQ:Z_MK - Z_MQ + HM * DK].rearrange("p (h d) -> p h d", d=DK)
                        pack(pool.tensor_scalar(kb[r, :, i * DK:(i + 1) * DK], src, DK ** -0.5, 1.0, ALU.mult, ALU.mult))
                    src = z_rec[:, Z_MV - Z_MQ:Z_MO - Z_MQ].rearrange("p (h d) -> p h d", d=DV)
                    pack(pool.tensor_copy(vaug[:, :, 0:DV], src))
                elif what == "cqT":
                    pool.wait_ge(in_ssq, 2 * (n + 1))
                    if n:
                        wait_read(pool, ("q1", n - 1))
                        pool.wait_ge(cn_ok, n)
                    rsqrt(rs_in, st_in, 1.0, in_rstd, n + 1)
                elif what == "ksum":
                    kv_rstd_of(n)
                elif what == "hsq":
                    pool.wait_ge(hs_ok, n + 1)
                    rsqrt(rs_m, st_m, 1.0 / DV, hr_ok, n + 1)
                elif what == "o1":
                    pool.wait_ge(x1_sq, n + 1)
                    rsqrt(rs_x, st_x, 1.0, x1_rs, n + 1)

            pool.wait_ge(wout_in, 16 * 8)
            for n in range(-1, NT + 1):
                for h in range(HA + 1):
                    for key in filler(n, h):
                        pool_work(key)

            pool.wait_ge(rec_ok, 2)
            pool.wait_ge(slots_clear, 16)
            for n in range(NT):
                for k in range(2):
                    pool.indirect_dma_start(slot_dram, bass.IndirectOffsetOnAxis(ap=rt_dest[:, k, n:n + 1], axis=0),
                                            rt["rec"][:, 2 * n + k, :], None, bounds_check=NSLOT - 1,
                                            oob_is_err=False).then_inc(rec_out, 16)
            pool.wait_ge(tab_ok, 1)
            pool.wait_ge(xn_out, 16 * NT)

            last_token = pool.to_reg(ROWS - 1)

            def gather(s, b, signal):
                pool.tensor_copy(now_tok[s][:], slot_tok[:, bass.ds(b, 1)]).then_inc(gather_idx, 1)
                pool.wait_ge(gather_idx, b + 1)
                pool.sem_inc(index_steps, 1)
                pool.indirect_dma_start(xe[s], None, xn_dram,
                                        bass.IndirectOffsetOnAxis(ap=now_tok[s][:], axis=0),
                                        bounds_check=last_token, oob_is_err=False).then_inc(signal, 16)

            def scatter(s, b, signal, before, count):
                pool.wait_ge(y_read, b + 1)
                pool.tensor_copy(now_out[s][:], slot_out[:, bass.ds(b, 1)]).then_inc(scatter_idx, 1)
                pool.wait_ge(before, count)
                pool.wait_ge(scatter_idx, b + 1)
                pool.sem_inc(index_steps, 1)
                pool.indirect_dma_start(O["y"], bass.IndirectOffsetOnAxis(ap=now_out[s][:], axis=0),
                                        ye[s], None, bounds_check=last_token, compute_op=ALU.add,
                                        oob_is_err=False).then_inc(signal, 16)

            for s in range(2):
                gather(s, s, xe_in[s])
            with pool.Fori(0, NE // 2 - 1) as j:
                for s in range(2):
                    b = 2 * j + s
                    pool.wait_ge(xeT_full, b + 1)
                    gather(s, b + 2, xe_in[s])
                    scatter(s, b, ye_out[s], ye_out[1 - s], 16 * (j + s))
            for s in range(2):
                scatter(s, NE - 2 + s, ye_out[s], ye_out[1 - s], 16 * (NE // 2 - 1 + s))
            total = pool.value_load(over_e[0:1, MAX_OVER:MAX_OVER + 1], min_val=0, max_val=MAX_OVER)
            pool.wait_ge(ye_out[1], 16 * (NE // 2))
            with pool.Fori(0, MAX_OVER) as j:
                with pool.If(j < total):
                    pool.wait_ge(xeT_full, NE + j)
                    gather(0, NE + j, ov_xe)
                    scatter(0, NE + j, ov_ye, ov_ye, 16 * j)
            pool.wait_ge(ye_out[0], 16 * (NE // 2))
            pool.wait_ge(ov_ye, 16 * total)

        @block.vector
        def _(dve):
            link = chain(dve, dve_link)
            TT, TS, STT = dve.tensor_tensor, dve.tensor_scalar, dve.scalar_tensor_tensor

            def kv_sums(m):
                st = st_qk[m % 2]
                dve.wait_ge(kn_sq, m + 1)
                dve.wait_ge(kr_ssq, m + 1)
                if m >= 2:
                    dve.wait_ge(kv_rstd, m - 1)
                link(dve.tensor_reduce(st[:, 8:16], sqk.rearrange("p (h d) -> p h d", d=NOPE), AX, ALU.add))
                TS(st[:, 8:16], st[:, 8:16], krss[m % 2], None, ALU.add).then_inc(kv_stats, 1)

            def kv_norm(m):
                rs = rs_qk[m % 2]
                wait_read(dve, ("kn", m))
                dve.wait_ge(kv_rstd, m + 1)
                if m >= 2:
                    wait_full(dve, ("kTb", m - 2))
                TT(kk[m % 2][:, :, 0:NOPE], kk[m % 2][:, :, 0:NOPE], bc(rs[:, 8:16], [P, HA, NOPE]), ALU.mult)
                TT(kk[m % 2][:, :, NOPE:], bc1(cn[m % 2][:, KL:], [P, HA, ROPE]), bc(rs[:, 8:16], [P, HA, ROPE]),
                   ALU.mult).then_inc(kk_ok, 1)

            for m in range(2):
                dve.memset(st_qk[m], 1.0).then_inc(stq_ok, 1)
            dve.wait_ge(stq_ok, 2)
            for c in range(NC):
                kv_sums(c)
                kv_norm(c)

            def xT_take(s, j, before_it=None):
                dve.wait_ge(xt_full[s], j + 1)
                if before_it is not None:
                    dve.wait_ge(z_full[3], before_it)
                TT(xT[s], bank(2 * s, 2).rearrange("p (k t) -> p k t", t=P), bc(g_attn, [P, KD, P]),
                   ALU.mult).then_inc(xt_read[s], 1)

            def z_take(s, n, j):
                dve.wait_ge(x_rstd[s], j + 1)
                dve.wait_ge(zst_out[s], 16 * j)
                for c in (1, 3):
                    lo, hi = Z_CHUNKS[c]
                    dve.wait_ge(z_full[c], n + 1)
                    TS(zst[s][:, lo:hi], bank(4 + c)[:, 0:hi - lo], xrs[s], None, ALU.mult).then_inc(z_read[c], 1)

            dve.wait_ge(const_in, 32)
            xT_take(0, 0)
            with dve.Fori(0, NT // 2) as j:
                xT_take(1, j, 2 * j)
                z_take(0, 2 * j, j)
                xT_take(0, j + 1, 2 * j + 1)
                z_take(1, 2 * j + 1, j)
            z_take(0, NT - 1, NT // 2)

            keep, negpad, cont, restart = [gate_rows[:, i] for i in range(4)]
            dve.memset(GQ, 0.0).then_inc(gq_zero, 1)
            dve.wait_ge(gate_in, 16)
            dve.wait_ge(mixw_in, 16 * 10)
            dve.wait_ge(s_full, 1)
            TS(gI, bank(0, 3)[0:HM, 0:ROWS], b_gate[:, 0:1], None, ALU.add).then_inc(s_read, 1)
            dve.wait_ge(s_full, 2)
            TS(gF, bank(0, 3)[0:HM, 0:ROWS], b_gate[:, 1:2], None, ALU.add).then_inc(s_read, 1)
            dve.wait_ge(g_a, 1)
            link(STT(gF, gF, 0.0, gA, ALU.min, ALU.subtract))
            link(TT(gF, gF, keep, ALU.mult))
            link(dve.tensor_tensor_scan(gB, cont, gF, 0.0, ALU.mult, ALU.add))
            link(TT(gI, gI, gB, ALU.subtract))
            link(TT(gI, gI, negpad, ALU.add))
            link(dve.tensor_tensor_scan(gM, restart, gI, 0.0, ALU.add, ALU.max))
            by_chunk = lambda a: a.rearrange("p (c t) -> p c t", t=CH)
            link(dve.tensor_copy(m_last, by_chunk(gM)[:, :, CH - 1]))
            link(dve.tensor_copy(b_last, by_chunk(gB)[:, :, CH - 1]))
            link(dve.tensor_tensor_scan(m_out[:, 1:], m_last[:, 1:], b_last[:, 1:], 0.0, ALU.max, ALU.add))
            link(STT(m_out[:, 0:1], m_last[:, 0:1], mstate, b_last[:, 0:1], ALU.max, ALU.add))
            link(dve.memset(m_prev[:, 1:2], 0.0))
            link(dve.tensor_copy(m_prev[:, 0:1], mstate))
            link(dve.tensor_copy(m_prev[:, 2:], m_out[:, 1:NCH - 1]))
            link(TT(by_chunk(gM), by_chunk(gM), bc(m_prev, [HM, NCH, CH]), ALU.max))
            link(dve.tensor_copy(m_last, by_chunk(gM)[:, :, CH - 1]))
            dve.wait_ge(gq_zero, 1)
            link(dve.tensor_copy(GQ[0:HM], gI))
            link(TT(by_chunk(GQ[32:32 + HM]), bc(m_prev, [HM, NCH, CH]), by_chunk(gM), ALU.subtract))
            link(TT(by_chunk(GQ[64:64 + HM]), by_chunk(gI), bc(m_last, [HM, NCH, CH]), ALU.subtract))
            link(TS(NM, gM, -1.0, None, ALU.mult))
            link(TT(GQ[96:96 + HM], NM, gB, ALU.subtract))
            TT(dec4, m_prev, m_last, ALU.subtract).then_inc(g_v, 1)
            link(TT(g_qk[:, 2:3], g_qk[:, 0:1], g_qk[:, 1:2], ALU.mult))
            TS(g_qk[:, 2:3], g_qk[:, 2:3], QK ** -0.5, None, ALU.mult).then_inc(g_qk_ok, 1)
            dve.wait_ge(s_full, 3)
            dve.tensor_copy(decb, bank(0)[:, 0:HM * NCH]).then_inc(s_read, 1)
            dve.wait_ge(s_read, 3)

            def rotate(x, n, lead, tmp):
                cos, sin = rope[:, n, 0], rope[:, n, 1]
                hr = ROPE // 2
                if lead:
                    cos = bc1(cos, [P, lead, ROPE])
                    s0, s1 = bc1(sin[:, 0:hr], [P, lead, hr]), bc1(sin[:, hr:], [P, lead, hr])
                    lo, hi, tl, th_ = x[:, :, 0:hr], x[:, :, hr:], tmp[:, :, 0:hr], tmp[:, :, hr:]
                else:
                    s0, s1 = sin[:, 0:hr], sin[:, hr:]
                    lo, hi, tl, th_ = x[:, 0:hr], x[:, hr:], tmp[:, 0:hr], tmp[:, hr:]
                link(TT(tl, hi, s0, ALU.mult))
                link(TT(th_, lo, s1, ALU.mult))
                link(TT(x, x, cos, ALU.mult))
                return lambda: TT(x, x, tmp, ALU.add)

            def fill_work(key):
                what, n = key
                if what == "cqT":
                    o = wait_full(dve, key)
                    if n:
                        wait_full(dve, ("q1", n - 1))
                    done_read(TT(cqT, o[:, 0:2 * P].rearrange("p (a b) -> p a b", b=P), bc(g_cq, [P, 2, P]), ALU.mult), key)
                    m = NC + n
                    dve.wait_ge(in_rstd, n + 1)
                    wait_full(dve, ("ckvT", m - 2))
                    dve.wait_ge(kr_ssq, m - 1)
                    if n >= 2:
                        dve.wait_ge(kv_out[n % 2], 32 * (n // 2))
                    z = z_lat
                    link(STT(cn[m % 2][:, 0:KL], z[:, Z_CKV:Z_CKV + KL], rs_in[:, 1:2], g_ckv, ALU.mult, ALU.mult))
                    kr = cn[m % 2][:, KL:]
                    link(dve.tensor_copy(kr, z[:, Z_KR:Z_KR + ROPE]))
                    rotate(kr, n, 0, ropet[:, 0:ROPE])().then_inc(cn_ok, 1)
                elif what == "qsum":
                    dve.wait_ge(q_sq, n + 1)
                    dve.wait_ge(kv_rstd, NC + n - 1)
                    dve.tensor_reduce(st_qk[(NC + n) % 2][:, 0:8], sqq, AX, ALU.add).then_inc(qs_ok, 1)
                    dve.wait_ge(qs_ok, n + 1)
                elif what == "ksum":
                    kv_sums(n)
                elif what == "kq":
                    kv_norm(n)
                    n -= NC
                    link(TT(qk, qk, bc(rs_qk[(NC + n) % 2][:, 0:8], [P, HA, QK]), ALU.mult))
                    rotate(qk[:, :, NOPE:], n, HA, sqq[:, :, 0:ROPE])().then_inc(q_ok, 1)
                elif what == "nm":
                    o = wait_full(dve, key)
                    wait_read(dve, ("gt", n))
                    if n:
                        dve.wait_ge(hs_ok, n)
                        wait_full(dve, ("nb", n - 1))
                    done_read(TT(Dm, o.rearrange("p (a b) -> p a b", b=P), bc(gt[:, 0:HM], [P, HM, P]), ALU.add), key)
                    wait_read(dve, key)
                    TT(Dm, Dm, bc1(chunk_mask, [P, HM, P]), ALU.add).then_inc(d_ok, 1)
                elif what == "kbT":
                    o = wait_full(dve, key)
                    done_read(dve.tensor_copy(kbT, o.rearrange("p (a b) -> p a b", b=P)), key)
                    dve.wait_ge(packed, 5 * (n + 1))
                    if n:
                        wait_full(dve, ("ub", n - 1))
                    TT(kw, kb, bc(gt[:, 64:64 + HM], [P, HM, P]), ALU.mult).then_inc(kw_ok, 1)
                elif what == "qkm":
                    o = wait_full(dve, key)
                    dve.wait_ge(e_ok, n + 1)
                    done_read(TT(Dm, Dm, o.rearrange("p (a b) -> p a b", b=P), ALU.mult), key)
                elif what in ("ua", "ub"):
                    o = wait_full(dve, key)
                    cur, nxt = state[n % 2], state[(n + 1) % 2]
                    h0 = 0 if what == "ua" else 2
                    if n:
                        wait_read(dve, ("ub", n - 1))
                    if n == 1:
                        dve.wait_ge(state_out, 16)
                    mid = cur if n else nxt
                    for h in range(h0, h0 + 2):
                        u = o[:, (h - h0) * CAUG:(h - h0 + 1) * CAUG]
                        dec = decb[0:DK, h * NCH + 2 * n:h * NCH + 2 * n + 1]
                        STT(mid[DK:P, h], cur[0:DK, h], dec, u[0:DK], ALU.mult, ALU.add).then_inc(st1_ok, 1)
                    dve.wait_ge(st1_ok, HM * n + h0 + 2)
                    for h in range(h0, h0 + 2):
                        u = o[:, (h - h0) * CAUG:(h - h0 + 1) * CAUG]
                        dec = decb[DK:P, h * NCH + 2 * n + 1:h * NCH + 2 * n + 2]
                        ins = STT(nxt[0:DK, h], cur[DK:P, h], dec, u[DK:P], ALU.mult, ALU.add)
                    done_read(ins, key)
                elif what in ("ia", "ib"):
                    o = wait_full(dve, key)
                    h0 = 0 if what == "ia" else 2
                    view = o[:, 0:2 * CAUG].rearrange("p (a b) -> p a b", b=CAUG)
                    if what == "ia" and n:
                        dve.wait_ge(h_ok, n)
                    done_read(TT(num[:, h0:h0 + 2], view, bc(gt[:, 32 + h0:34 + h0], [P, 2, CAUG]), ALU.mult), key)
                    wait_read(dve, key)
                elif what in ("na", "nb"):
                    o = wait_full(dve, key)
                    h0 = 0 if what == "na" else 2
                    view = o[:, 0:2 * CAUG].rearrange("p (a b) -> p a b", b=CAUG)
                    done_read(TT(num[:, h0:h0 + 2], num[:, h0:h0 + 2], view, ALU.add), key)
                    if what == "nb":
                        mlstm_ratio(n)
                elif what == "hsq":
                    dve.wait_ge(hsq_ok, n + 1)
                    dve.tensor_reduce(st_m, Dm, AX, ALU.add).then_inc(hs_ok, 1)
                    dve.wait_ge(og_ok, n + 1)
                    link(STT(og, og, 1.0, g_mh, ALU.add, ALU.mult))
                elif what == "hout":
                    dve.wait_ge(hr_ok, n + 1)
                    link(TT(hm, hm, bc(rs_m, [P, HM, DV]), ALU.mult))
                    if n:
                        wait_full(dve, ("mxb", n - 1))
                    STT(mix[:, BANK:], hm.rearrange("p a b -> p (a b)"), 0.5, og, ALU.mult,
                        ALU.mult).then_inc(mm_ok, 1)
                elif what == "mxb":
                    o = wait_full(dve, key)
                    if n:
                        wait_full(dve, ("lg", n - 1))
                    done_read(dve.tensor_copy(mixT[:, 4:8], o.rearrange("p (a b) -> p a b", b=P)), key)
                elif what in ("o0", "o1"):
                    o = wait_full(dve, key)
                    dve.wait_ge(xres_in, 16 * (n + 1))
                    lo = 0 if what == "o0" else BANK
                    done_read(TT(xres[:, lo:lo + BANK], xres[:, lo:lo + BANK], o, ALU.add), key)
                elif what == "xnorm":
                    dve.wait_ge(x1_rs, n + 1)
                    STT(xn, xres, rs_x, g_ffn, ALU.mult, ALU.mult).then_inc(xn_ok, 1)
                elif what == "xnb":
                    o = wait_full(dve, key)
                    wait_full(dve, ("o1", n))
                    done_read(dve.tensor_copy(xnT[:, 4:8], o.rearrange("p (a b) -> p a b", b=P)), key)
                elif what == "lg":
                    o = wait_full(dve, key)
                    done_read(TT(logits[:, n], o[:, 0:NG + NE], b_route, ALU.add), key)

            def mlstm_ratio(n):
                wait_read(dve, ("na", n))
                wait_read(dve, ("nb", n))
                link(STT(den[:, 0:HM], num[:, :, DV], -1.0, num[:, :, DV], ALU.mult, ALU.max))
                link(TT(den[:, 0:HM], den[:, 0:HM], gt[:, 96:96 + HM], ALU.max))
                link(dve.reciprocal(den[:, HM:], den[:, 0:HM]))
                if n:
                    dve.wait_ge(mm_ok, n)
                TT(hm, num[:, :, 0:DV], bc(den[:, HM:], [P, HM, DV]), ALU.mult).then_inc(h_ok, 1)

            def row_max(n, h):
                q = DEC if n == 0 else P
                last = key_blocks(n)[-1]
                dve.wait_ge(s_full, 4 + n * HA + h)
                o = bank(0, 3)
                if n:
                    link(dve.memset(o[0:CH, last[0] - CH:last[0]], NEG))
                dve.tensor_reduce(nmax[0:q, h:h + 1], o[0:q, 0:last[0] + last[3]], AX, ALU.max,
                                  negate=True).then_inc(max_ok, 1)

            def pT_take(n, h):
                q = DEC if n == 0 else P
                blocks = key_blocks(n)
                for g in range(0, (len(blocks) + 3) // 4, 2):
                    key = ("pT", n, h, g)
                    o = wait_full(dve, key)
                    wait_values(dve, n, h)
                    take_pT(dve.tensor_copy, o, blocks[4 * g:4 * g + 4], 4 * g, q, key)

            def attention_out(n):
                q = DEC if n == 0 else P
                dve.wait_ge(s_read, 3 + (n + 1) * HA)
                link(dve.reciprocal(rinv[0:q], rsum[0:q]))
                dve.wait_ge(pv_done, (n + 1) * HA)
                if n:
                    wait_full(dve, ("mxb", n - 1))
                TT(mix[0:q, 0:BANK].rearrange("p (h d) -> p h d", d=VD),
                   bank(4)[0:q].rearrange("p (h d) -> p h d", d=VD), bc(rinv[0:q], [q, HA, VD]),
                   ALU.mult).then_inc(o_read, 1)

            dve.wait_ge(wout_in, 16 * 8)
            link(dve.memset(mix[DEC:P, 0:BANK], 0.0))
            for n in range(-1, NT + 1):
                now = 0 <= n < NT
                if now:
                    row_max(n, 0)
                for h in range(HA):
                    for key in filler(n, h):
                        fill_work(key)
                    if now:
                        pT_take(n, h)
                        if h + 1 < HA:
                            row_max(n, h + 1)
                for key in filler(n, HA):
                    fill_work(key)
                if now:
                    attention_out(n)

            iota, first, over_j = route_rows[:, 0:NE], route_rows[:, NE:2 * NE], route_rows[:, 2 * NE:2 * NE + MAX_OVER]
            tok_rows = route_rows[:, 5 * NE:5 * NE + 2 * NT].rearrange("p (k n) -> p k n", n=NT)
            nowhere = route_rows[:, 5 * NE + 2 * NT:5 * NE + 3 * NT]
            R = rt
            col = lambda i: R["cols"][:, i]
            e32 = [P, NT, NE]
            for b in range(4):
                dve.wait_ge(read[b], ring_used[b])
            dve.wait_ge(x1_out, 16 * NT)
            dve.wait_ge(xn_out, 16 * NT)

            def pick_first(scores_, top, width, index, one_hot):
                shape = [P, NT, width]
                link(TT(one_hot, scores_, bc(top, shape), ALU.is_equal))
                link(STT(one_hot, one_hot, -64.0, bc1(index, shape), ALU.mult, ALU.add))
                link(dve.tensor_reduce(col(15), one_hot, AX, ALU.min))
                link(TT(one_hot, one_hot, bc(col(15), shape), ALU.is_equal))

            gl = logits[:, :, 0:NG]
            link(dve.tensor_reduce(col(0), gl, AX, ALU.max))
            pick_first(gl, col(0), NG, iota[:, 0:NG], R["goh"])
            link(TT(R["ge"], gl, bc(col(0), [P, NT, NG]), ALU.subtract))
            link(TS(R["goh"], R["goh"], -NEG, NEG, ALU.mult, ALU.add))
            link(TT(R["el"].rearrange("p n (g e) -> p n g e", e=EG),
                    logits[:, :, NG:].rearrange("p n (g e) -> p n g e", e=EG), bc(R["goh"], [P, NT, NG, EG]), ALU.add))
            link(dve.tensor_reduce(col(1), R["el"], AX, ALU.max))
            pick_first(R["el"], col(1), NE, iota, R["oh1"])
            link(STT(R["el"], R["oh1"], 2e8 * NEG, R["el"], ALU.mult, ALU.add))
            link(dve.tensor_reduce(col(2), R["el"], AX, ALU.max))
            pick_first(R["el"], col(2), NE, iota, R["oh2"])
            link(TT(col(6), col(2), col(1), ALU.subtract))
            for oh in ("oh1", "oh2"):
                link(dve.memset(R[oh][DEC:P, 0], 0.0))
            link(TT(R["m"], R["oh1"], R["oh2"], ALU.add))
            link(dve.memset(R["mp"][:, 0], 0.0))
            for n in range(NT):
                ins = TT(R["mp"][:, n + 1], R["mp"][:, n], R["m"][:, n], ALU.add)
                if n < NT - 1:
                    link(ins)
            ins.then_inc(r_dve, 1)
            dve.wait_ge(r_act, 2)
            link(dve.tensor_reduce(col(3), R["ge"], AX, ALU.add))
            link(TS(col(4), col(6), 1.0, None, ALU.add))
            link(TT(col(5), col(3), col(4), ALU.mult))
            link(dve.reciprocal(col(7), col(5)))
            link(TT(col(8), col(7), col(6), ALU.mult))
            dve.wait_ge(r_pe, 1)
            link(dve.tensor_copy(R["rank"], bank(0)[:, 0:NT * NE].rearrange("p (a b) -> p a b", b=NE)))
            link(dve.tensor_copy(R["cnt"], bank(1)[:, 0:NE]))
            link(TS(R["ov"], R["cnt"], float(P), None, ALU.is_gt))
            for k in range(2, (TOKENS + P - 1) // P):
                link(STT(R["ov"], R["cnt"], float(k * P), R["ov"], ALU.is_gt, ALU.add))
            link(dve.memset(R["base"], 1.0))
            link(dve.tensor_tensor_scan(R["ovend"], R["base"], R["ov"], 0.0, ALU.mult, ALU.add))
            link(TT(R["base"], R["ovend"], R["ov"], ALU.subtract))
            link(TS(R["base"], R["base"], float(P), float((NE - 1) * P), ALU.mult, ALU.add))
            link(TT(R["base"], R["base"], first, ALU.subtract))
            link(TS(R["far"], R["rank"], float(P), None, ALU.is_ge))
            link(TT(R["far"], R["far"], bc1(R["base"], e32), ALU.mult))
            link(TT(R["pos"], R["rank"], bc1(first, e32), ALU.add))
            link(TT(R["pos"], R["pos"], R["far"], ALU.add))
            for k, oh in enumerate(("oh1", "oh2")):
                link(TT(R["t"], R[oh], R["pos"], ALU.mult))
                link(dve.tensor_reduce(col(9 + k), R["t"], AX, ALU.add))
                link(TT(col(9 + k), col(9 + k), nowhere, ALU.add))
                link(dve.tensor_copy(rt_dest[:, k], col(9 + k)))
            rec = R["rec"].rearrange("p (n k) c -> p n k c", k=2)
            for k in range(2):
                link(dve.tensor_copy(rec[:, :, k, 0], tok_rows[:, 0]))
                link(dve.tensor_copy(rec[:, :, k, 1], tok_rows[:, k]))
                link(dve.tensor_copy(rec[:, :, k, 2], col(7 + k)))
                dve.tensor_copy(rec[:, :, k, 3], col(7 + k)).then_inc(rec_ok, 1)
            cmp = R["cmp"][0:1]
            shape = [1, MAX_OVER, NE]
            link(TT(cmp, bc1(R["ovend"][0:1], shape), bc(over_j[0:1], shape), ALU.is_le))
            link(dve.tensor_reduce(R["over"][0:1, 0:MAX_OVER], cmp, AX, ALU.add))
            link(TS(R["over"][0:1, 0:MAX_OVER], R["over"][0:1, 0:MAX_OVER], float(NE - 1), None, ALU.min))
            link(dve.tensor_copy(R["over"][0:1, MAX_OVER:], R["ovend"][0:1, NE - 1:NE]))
            link(dve.tensor_copy(over_e[:], R["over"][0:1]))
            dve.wait_ge(rec_in, 16)
            link(dve.tensor_copy(slot_tok[:], slot_rec[:, :, 0]))
            dve.tensor_copy(slot_out[:], slot_rec[:, :, 1]).then_inc(tab_ok, 1)

            def xeT_take(s, b):
                dve.wait_ge(xeT_full, b + 1)
                dve.tensor_copy(xeT[s], bank(0, 2).rearrange("p (k t) -> p k t", t=P)).then_inc(xeT_read, 1)

            def hidden(s, b):
                dve.wait_ge(tanh_ok, b + 1)
                STT(uu, th, 1.0, bank(2), ALU.add, ALU.mult).then_inc(u_ok, 1)
                dve.wait_ge(u_ok, b + 1)
                dve.wait_ge(h3_full, b + 1)
                dve.wait_ge(hT_full, b)
                STT(hh, uu, 0.5, bank(3), ALU.mult, ALU.mult).then_inc(hh_ok, 1)

            def hT_take(b):
                dve.wait_ge(hT_full, b + 1)
                dve.wait_ge(y_full, b)
                dve.tensor_copy(hT, bank(4).rearrange("p (k t) -> p k t", t=P)).then_inc(hT_read, 1)

            xeT_take(0, 0)
            with dve.Fori(0, NE // 2 - 1) as j:
                for s in range(2):
                    hidden(s, 2 * j + s)
                    xeT_take(1 - s, 2 * j + s + 1)
                    hT_take(2 * j + s)
            hidden(0, NE - 2)
            xeT_take(1, NE - 1)
            hT_take(NE - 2)
            hidden(1, NE - 1)
            hT_take(NE - 1)
            total = dve.value_load(over_e[0:1, MAX_OVER:MAX_OVER + 1], min_val=0, max_val=MAX_OVER)
            with dve.Fori(0, MAX_OVER) as j:
                with dve.If(j < total):
                    xeT_take(0, NE + j)
                    hidden(0, NE + j)
                    hT_take(NE + j)


def kernel(**inputs):
    import numpy as _np
    import concourse.bacc as _bacc
    from concourse.bass_utils import run_bass_kernel_spmd as _run

    a = {k: _np.asarray(v)[0] if k not in ("x_prompt", "x_sample", "meta_tokens") else _np.asarray(v)
         for k, v in inputs.items()}
    x = _np.zeros((ROWS, D), _np.float32)
    x[:DEC] = a["x_sample"][0]
    x[DEC:DEC + META] = a["meta_tokens"]
    x[P:] = a["x_prompt"][0]
    w = a["w_in"]
    gates = QL + KL + ROPE + 2 * HM * DK + HM * DV
    first = QL + KL + ROPE
    cols = [w[:, :first], w[:, gates:gates + 2 * HM], w[:, first:gates], w[:, gates + 2 * HM:]]
    ukv = a["w_ukv"].reshape(KL, HA, NOPE + VD)
    host = {
        "x_rows": x,
        "cache_ckv": a["cache_ckv"][0],
        "cache_kr": a["cache_krope"][0],
        "state_c": _np.concatenate([a["state_mlstm_c"][0].transpose(2, 0, 1),
                                    a["state_mlstm_n"][0].T[:, :, None]], axis=2).reshape(DK, HM * CAUG),
        "state_m": a["state_mlstm_m"].reshape(HM, 1),
        "g_attn": a["g_attn"].reshape(KD, P).T,
        "w_in": _np.concatenate(cols, axis=1),
        "g_cq": a["g_cq"].reshape(QL // P, P).T,
        "w_uq": a["w_uq"].reshape(QL, HA * QK),
        "g_ckv": a["g_ckv"][None],
        "w_ukv": _np.concatenate([ukv[:, :, :NOPE].reshape(KL, -1), ukv[:, :, NOPE:].reshape(KL, -1)], axis=1),
        "g_q": a["g_q"][:, None],
        "g_k": a["g_k"][:, None],
        "b_gate": _np.stack([a["b_igate"], a["b_fgate"]], axis=1),
        "g_mh": a["g_mh"].reshape(1, HM * DV),
        "w_out": a["w_out"],
        "g_ffn": a["g_ffn"][None],
        "w_route": _np.concatenate([a["w_group"], a["w_erouter"]], axis=1),
        "b_route": _np.concatenate([a["b_group"], a["b_erouter"]])[None],
        "w1": a["w1"], "w3": a["w3"], "w2": a["w2"],
    }
    nc = _bacc.Bacc("TRN2", target_bir_lowering=False, num_devices=1)
    T, O, arrays = {}, {}, {}
    for name, array in {**host, **CONSTS}.items():
        array = _np.ascontiguousarray(array)
        assert array.shape == INS.get(name, array.shape), (name, array.shape)
        arrays["in_" + name] = array
        T[name] = nc.dram_tensor("in_" + name, array.shape, mybir.dt.from_np(array.dtype), kind="ExternalInput").ap()
    for name, shape in OUTS.items():
        O[name] = nc.dram_tensor("out_" + name, shape, F32, kind="ExternalOutput").ap()
    build(nc, T, O)
    r = _run(nc, [arrays], core_ids=[0]).results[0]
    o = {name: _np.asarray(r["out_" + name]) for name in OUTS}

    def state_of(s):
        s = s.reshape(DK, HM, CAUG).transpose(1, 2, 0)
        return s[None, None, :, :DV], s[None, None, :, DV]

    c_p, n_p = state_of(o["c_prompt"])
    c_s, n_s = state_of(o["c_sample"])
    return (o["y"][None, P:], o["y"][None, :DEC], o["ckv"][None, None, DEC:][:, :, list(range(META)) + list(range(P - DEC, ROWS - DEC))],
            o["krope"][None, None, DEC:][:, :, list(range(META)) + list(range(P - DEC, ROWS - DEC))], c_p, n_p,
            o["m_both"][None, None, 0, :, 0], o["ckv"][None, None, :DEC], o["krope"][None, None, :DEC], c_s, n_s,
            o["m_both"][None, None, 1, :, 0])
```

```python
from contextlib import ExitStack

import numpy as np

import concourse.bass as bass
from concourse import mybir

F32 = mybir.dt.float32
U32 = mybir.dt.uint32
I32 = mybir.dt.int32
ALU = mybir.AluOpType
ACT = mybir.ActivationFunctionType
AX = mybir.AxisListType.X

P = 128
D = 1024
KD = D // P
SEQ, DEC, META, PAST = 1024, 64, 16, 1024
NT = 1 + SEQ // P
NC = PAST // P
ROWS = NT * P
CH = 64
NCH = ROWS // CH
HA, NOPE, ROPE, VD = 8, 64, 32, 64
QK = NOPE + ROPE
QL, KL = 256, 128
HM, DK, DV = 4, 64, 128
CAUG = DV + 1
EPS = 1e-6
NG, EG = 4, 8
NE = NG * EG
FF = 512
KF = FF // P
Z_CQ, Z_CKV, Z_KR, Z_GATE, Z_MQ, Z_MK, Z_MV, Z_MO = 0, 256, 384, 416, 424, 680, 936, 1448
ZW = 1960
Z_CHUNKS = [(0, 424), (424, 936), (936, 1448), (1448, 1960)]
SLOTS = NT + 1
BANK = 512
NEG = -1.0e30
TOKENS = SEQ + DEC
MAX_OVER = (2 * TOKENS - 2) // P
NBLK = NE + MAX_OVER
ROUTE_W = P + NE + MAX_OVER + 2 * NT
NOWHERE = 1.0e6


def constants():
    c = {}
    c["ident"] = np.eye(P, dtype=np.float32)
    s, t = np.meshgrid(np.arange(P), np.arange(P), indexing="ij")
    c["chunk_mask"] = np.where((s // CH == t // CH) & (s <= t), 0.0, NEG).astype(np.float32)
    c["before"] = (s < t).astype(np.float32)
    pos = np.zeros(ROWS)
    pos[:DEC] = PAST + np.arange(DEC)
    pos[DEC:DEC + META] = np.arange(META) - META
    pos[P:] = np.arange(SEQ)
    half = ROPE // 2
    inv = np.float32(10000.0) ** (-np.arange(half, dtype=np.float32) / np.float32(half))
    ang = pos.astype(np.float32)[:, None] * inv[None, :].astype(np.float32)
    cos, sin = np.cos(ang).astype(np.float32), np.sin(ang).astype(np.float32)
    table = np.concatenate([cos, cos, -sin, sin], axis=1).reshape(NT, P, 2 * ROPE)
    c["rope"] = np.ascontiguousarray(table.transpose(1, 0, 2).reshape(P, NT * 2 * ROPE))
    keep = np.ones(ROWS, np.float32)
    keep[DEC + META:P] = 0.0
    start = (np.arange(ROWS) % CH == 0)
    rows = [keep, np.where(keep > 0, 0.0, NEG), np.where(start, 0.0, 1.0), np.where(start, 3 * NEG, 0.0)]
    c["gate_rows"] = np.broadcast_to(np.stack(rows).astype(np.float32)[None], (HM, 4, ROWS)).reshape(HM, 4 * ROWS).copy()
    sel = np.zeros((HM, HM, P), np.float32)
    for h in range(HM):
        sel[h, h] = 1.0
    c["pick_head"] = sel.reshape(HM, HM * P)
    ro = np.zeros((P, ROUTE_W), np.float32)
    ro[:, 0:P] = np.arange(P)
    ro[:, P:P + NE] = NE - 1 - np.arange(NE)
    ro[:, P + NE:P + NE + MAX_OVER] = np.arange(MAX_OVER)
    at = P + NE + MAX_OVER
    ro[:, at:at + NT] = np.arange(NT)[None, :] * P + np.arange(P)[:, None]
    ro[DEC:, at + NT] = NOWHERE
    c["route_rows"] = ro
    return c


CONSTS = constants()
INS = {
    "x_rows": (ROWS, D), "cache_ckv": (PAST, KL), "cache_kr": (PAST, ROPE), "state_c": (DK, HM * CAUG),
    "state_m": (HM, 1), "g_attn": (P, KD), "w_in": (D, ZW), "g_cq": (P, QL // P), "w_uq": (QL, HA * QK),
    "g_ckv": (1, KL), "w_ukv": (KL, 2 * HA * VD), "g_q": (QK, 1), "g_k": (QK, 1), "b_gate": (HM, 2),
    "g_mh": (1, HM * DV), "w_out": (D, D), "g_ffn": (1, D), "w_route": (D, NG + NE), "b_route": (1, NG + NE),
    "w1": (NE, D, FF), "w3": (NE, D, FF), "w2": (NE, FF, D),
}
OUTS = {
    "y": (ROWS, D), "ckv": (ROWS, KL), "krope": (ROWS, ROPE), "c_prompt": (DK, HM * CAUG),
    "c_sample": (DK, HM * CAUG), "m_both": (2, HM, 1),
}


def key_blocks(n):
    if n == 0:
        return [(i * P, 2 + i, 0, P) for i in range(NC)] + [(NC * P, 0, 0, DEC + META)]
    return [(i * P, 1 + i, 0, P) for i in range(n)] + [(n * P, 0, DEC, META)]


def cache_step(c):
    return ([("ckvT", c)] * (c < NC) + [("kn", c - 1), ("v", c - 1)] * (1 <= c <= NC)
            + [("kTa", c - 2), ("kTb", c - 2)] * (c >= 2))


def pe_fills():
    order = []
    for c in range(NC + 2):
        order += cache_step(c)
    for n in range(-1, NT + 1):
        for h in range(HA):
            order += [key for key in filler(n, h) if key[0] not in NO_BANK]
            if 0 <= n < NT:
                order += [("pT", n, h, g) for g in range((len(key_blocks(n)) + 3) // 4)]
        order += [key for key in filler(n, HA) if key[0] not in NO_BANK]
    fills, used = {}, [0, 0, 0, 0]
    for i, key in enumerate(order):
        assert key not in fills, key
        fills[key] = (i % 4, used[i % 4])
        used[i % 4] += 1
    return fills, used


def filler(n, h):
    now, nxt, old = 0 <= n < NT, n + 1 < NT, n >= 1
    m = NC + n + 1
    return {
        0: [("mxa", n - 1), ("mxb", n - 1)] * old + [("gt", n), ("nm", n)] * now,
        1: [("o0", n - 1)] * old + [("cqT", n + 1)] * nxt,
        2: [("o1", n - 1)] * old + [("qbT", n), ("kbT", n)] * now + [("ckvT", m)] * nxt,
        3: [("q0", n + 1), ("q1", n + 1)] * nxt + [("qkm", n), ("ua", n), ("ub", n)] * now + [("xnorm", n - 1)] * old,
        4: [("kn", m), ("v", m)] * nxt + [("ia", n), ("na", n)] * now + [("qsum", n + 1)] * nxt + [("ksum", m)] * nxt,
        5: [("ib", n), ("nb", n)] * now + [("xna", n - 1), ("xnb", n - 1)] * old + [("hsq", n)] * now,
        6: [("kq", m)] * nxt + [("lg", n - 1)] * old,
        7: [("qTa", n + 1), ("qTb", n + 1)] * nxt + [("hout", n)] * now,
        8: [("kTa", m), ("kTb", m)] * nxt,
    }[h]


NO_BANK = ("xnorm", "qsum", "hsq", "ksum", "kq", "hout")


def build(nc, T, O):
    ctx = ExitStack()
    with ctx:
        def sb(name, shape, dt=F32):
            return ctx.enter_context(nc.sbuf_tensor(name, shape, dt))

        def sem(name):
            return ctx.enter_context(nc.semaphore(name))

        z_dram = nc.dram_tensor("z_rows", (ROWS, ZW), F32, kind="Internal").ap()
        xn_dram = nc.dram_tensor("xn_rows", (ROWS, D), F32, kind="Internal").ap()

        psum = ctx.enter_context(nc.psum_tensor("psum", [P, 8 * BANK], F32))

        def bank(b, n=1):
            return psum[:, b * BANK:(b + n) * BANK]

        ident = sb("ident", [P, P])
        ones = sb("ones", [P, P])
        before = sb("before", [P, P])
        route_rows = sb("route_rows", [P, ROUTE_W])
        logits = sb("logits", [P, NT, NG + NE])
        slot_gate = sb("slot_gate", [P, NBLK])
        slot_tok = sb("slot_tok", [P, NBLK], U32)
        slot_out = sb("slot_out", [P, NBLK], U32)
        now_tok = [sb(f"now_tok{i}", [P, 1], U32) for i in range(2)]
        now_out = [sb(f"now_out{i}", [P, 1], U32) for i in range(2)]
        over_e = sb("over_e", [1, MAX_OVER + 1], I32)
        small = sb("small", [P, 512])
        arena = sb("arena", [P, 51400])

        class Area:
            def __init__(self, at=0):
                self.at = at

            def __call__(self, *shape, parts=P):
                n = int(np.prod(shape))
                a = arena[0:parts, self.at:self.at + n]
                self.at += n + n % 2
                assert self.at <= 51400, self.at
                if len(shape) == 2:
                    a = a.rearrange("p (a b) -> p a b", b=shape[1])
                if len(shape) == 3:
                    a = a.rearrange("p (a b c) -> p a b c", b=shape[1], c=shape[2])
                return a

        A = Area()
        KT = A(HA, SLOTS * P, parts=QK)
        V = A(SLOTS, HA * VD)
        Vmeta = A(HA * VD, parts=META)
        w_ukv = A(2 * HA * VD)
        cn = [A(KL + ROPE) for _ in range(2)]
        ckvT = [A(P) for _ in range(2)]
        kk = [A(HA, QK) for _ in range(2)]
        sqk = A(HA * NOPE)
        kjunk = A(KL)
        gat = A(NT, 2 * HM)
        GQ = A(ROWS)
        rope = A(NT, 2, ROPE)
        NM = arena[QK:QK + HM, 0:ROWS]
        pick = arena[QK:QK + HM, ROWS:ROWS + HM * P].rearrange("p (a b) -> p a b", b=P)
        dec4 = arena[QK:QK + HM, ROWS + HM * P:ROWS + HM * P + NCH]
        shared = A.at
        A = Area(shared)
        w_in = A(KD, ZW)
        xin = [A(D) for _ in range(2)]
        xT = [A(KD, P) for _ in range(2)]
        zst = [A(ZW) for _ in range(2)]
        junk = A(D)
        cached = zst[1][:, 0:NC * (KL + ROPE)].rearrange("p (c a) -> p c a", c=NC)
        A = Area(shared)
        w_out = A(KD, D)
        after_w_out = A.at
        w_uq = A(2, HA * QK)
        w_route = A(KD, NG + NE)
        z_lat = A(Z_MQ)
        z_rec = A(ZW - Z_MQ)
        cqT = A(2, P)
        qk = A(HA, QK)
        sqq = A(HA, QK)
        qT = [A(HA, P, parts=QK) for _ in range(2)]
        g_ckv = A(KL)
        after_queries = A.at
        probs = A(NT * P)
        pT = A(NT, P)
        mix = A(D)
        mixT = A(KD, P)
        xnT = mixT
        gt = A(P)
        Dm = A(HM, P)
        chunk_mask = A(P)
        qb, kb = A(HM, P), A(HM, P)
        kw = kb
        qbT, kbT = A(HM, P), A(HM, P)
        vaug = A(HM, CAUG)
        state = [A(HM, CAUG) for _ in range(2)]
        num = A(HM, CAUG)
        og = A(HM * DV)
        hm = A(HM, DV)
        g_mh = A(HM * DV)
        g_ffn = A(D)
        xres = A(D)
        xn = A(D)
        A = Area(after_queries)
        gate_rows = A(4, ROWS, parts=HM)
        gI, gF, gA, gB, gM = [A(ROWS, parts=HM) for _ in range(5)]
        A = Area(0)
        rt = {k: A(*s) for k, s in {
            "el": (NT, NE), "t": (NT, NE), "oh1": (NT, NE), "oh2": (NT, NE), "m": (NT, NE), "mp": (NT + 1, NE),
            "gt": (NT, NG), "goh": (NT, NG), "ge": (NT, NG), "rank": (NT, NE), "cnt": (NE,), "ov": (NE,),
            "ovend": (NE,), "base": (NE,), "cmp": (MAX_OVER, NE), "cols": (20, NT), "over": (MAX_OVER + 1,),
            "out": (NBLK,), "rows": (2 * NT, P), "blocks": (2 * NT, 3 * NBLK)}.items()}
        assert A.at <= HA * SLOTS * P
        w1s = [A(KD, FF) for _ in range(2)]
        w3s = [A(KD, FF) for _ in range(2)]
        w2s = [A(KF, D) for _ in range(2)]
        xe = [A(D) for _ in range(2)]
        xeT = [A(KD, P) for _ in range(2)]
        th = A(FF)
        uu = A(FF)
        hh = A(FF)
        hT = A(KF, P)
        ye = [A(D) for _ in range(2)]
        sp = [0]

        def tiny(n, parts=P):
            a = small[0:parts, sp[0]:sp[0] + n]
            sp[0] += n
            assert sp[0] <= 512
            return a
        xss = [tiny(1) for _ in range(2)]
        xrs = [tiny(1) for _ in range(2)]
        g_attn = tiny(KD)
        g_cq = tiny(2)
        g_qk = tiny(3, QK)
        b_gate = tiny(2, HM)
        mstate = tiny(1, HM)
        half = tiny(16)
        eps = tiny(1)
        st_in = tiny(2)
        rs_in = tiny(2)
        krss = [tiny(1) for _ in range(2)]
        st_qk = [tiny(16) for _ in range(2)]
        rs_qk = [tiny(16) for _ in range(2)]
        nmax = tiny(HA)
        rsum = tiny(HA)
        rinv = tiny(HA)
        ropet = tiny(2 * ROPE)
        den = tiny(2 * HM)
        st_m = tiny(HM)
        rs_m = tiny(HM)
        st_x = tiny(1)
        rs_x = tiny(1)
        m_out = tiny(NCH, HM)
        m_prev = tiny(NCH, HM)
        m_last = tiny(NCH, HM)
        b_last = tiny(NCH, HM)
        decb = tiny(HM * NCH)
        b_route = tiny(NG + NE)

        fills, ring_used = pe_fills()
        RB = [3, 5, 6, 7]
        full = [sem(f"ring{i}_full") for i in range(4)]
        read = [sem(f"ring{i}_read") for i in range(4)]
        s_full, s_read = sem("scores_full"), sem("scores_read")
        pv_done, o_read = sem("values_summed"), sem("att_read")
        xt_full = [sem(f"xT{i}_full") for i in range(2)]
        xt_read = [sem(f"xT{i}_read") for i in range(2)]
        z_full = [sem(f"z{i}_full") for i in range(4)]
        z_read = [sem(f"z{i}_read") for i in range(4)]
        x_in = [sem(f"x{i}_in") for i in range(2)]
        rs_mid = [sem(f"x{i}_mean") for i in range(2)]
        zst_out = [sem(f"z_store{i}") for i in range(2)]
        x_ssq = [sem(f"x{i}_ssq") for i in range(2)]
        x_rstd = [sem(f"x{i}_rstd") for i in range(2)]
        kvw_in, const_in, win_in = sem("w_ukv_in"), sem("const_in"), sem("w_in_in")
        cache_in = sem("cache_in")
        gate_in, mixw_in, wout_in = sem("gate_rows_in"), sem("mix_weights_in"), sem("w_out_in")
        wuq_in = sem("w_uq_in")
        zl_in, zr_in = sem("z_latents_in"), sem("z_mlstm_in")
        xres_in = sem("xres_in")
        kv_out = [sem(f"kv_store{i}") for i in range(2)]
        x1_out, xn_out = sem("x1_store"), sem("xn_store")
        state_out, m_store = sem("state_store"), sem("m_store")
        vmeta_in = sem("vmeta_in")
        half_ok = sem("half_ready")
        ones_ok = sem("ones_ready")
        kr_ssq = sem("kr_squares")
        kn_sq = sem("kn_squares")
        kv_stats = sem("qk_sums_ready")
        kv_rstd = sem("qk_rstd_ready")
        cn_ok = sem("ckv_kr_ready")
        in_ssq = sem("cq_ckv_sums")
        in_rstd = sem("cq_ckv_rstd")
        q_sq = sem("q_squares")
        q_ok = sem("q_ready")
        kk_ok = sem("k_ready")
        g_a, g_v, g_ok, g_qk_ok = sem("gate_logs"), sem("gate_dve"), sem("gate_exps"), sem("g_qk_ready")
        gq_zero, stq_ok, qs_ok = sem("gate_rows_zeroed"), sem("sums_preset"), sem("q_sums_ready")
        zero_ok = sem("mlstm_zeroed")
        packed = sem("mlstm_packed")
        d_ok, e_ok, kw_ok = sem("decay_logs"), sem("decay_exps"), sem("kw_ready")
        st1_ok = sem("state_mid")
        og_ok = sem("ogate_tanh")
        h_ok, hsq_ok, hs_ok, hr_ok = sem("h_ready"), sem("h_squares"), sem("h_sums"), sem("h_rstd")
        mm_ok = sem("mix_mlstm")
        max_ok = sem("scores_max")
        x1_sq, x1_rs, xn_ok = sem("res_squares"), sem("res_rstd"), sem("xn_ready")
        dve_link, act_link, pool_link = sem("dve_link"), sem("act_link"), sem("pool_link")
        r_dve, r_act, r_pe = sem("route_dve"), sem("route_act"), sem("route_pe")
        hot_ok = sem("slot_one_hots")
        index_steps = sem("index_steps")
        tab_ok, gather_idx, scatter_idx = sem("slot_tables_ready"), sem("gather_indices"), sem("scatter_indices")
        w1_in, w3_in, w2_in = [[sem(f"expert_{w}_{i}_in") for i in range(2)] for w in ("w1", "w3", "w2")]
        xe_in = [sem(f"xe{i}_in") for i in range(2)]
        xeT_full, xeT_read = sem("xeT_full"), sem("xeT_read")
        h1_full, h3_full = sem("h1_full"), sem("h3_full")
        tanh_ok, hh_ok = sem("silu_tanh"), sem("hh_ready")
        u_ok = sem("silu_ready")
        hT_full, hT_read = sem("hT_full"), sem("hT_read")
        y_full, y_read = sem("y_full"), sem("y_read")
        ye_out = [sem(f"ye{i}_store") for i in range(2)]
        ov_w, ov_xe, ov_ye = sem("over_w_in"), sem("over_xe_in"), sem("over_ye_store")

        block = ctx.enter_context(nc.Block())

        def wait_full(eng, key):
            b, k = fills[key]
            eng.wait_ge(full[b], k + 1)
            return bank(RB[b])

        def wait_read(eng, key):
            b, k = fills[key]
            eng.wait_ge(read[b], k + 1)

        def done_read(ins, key):
            ins.then_inc(read[fills[key][0]], 1)

        def chain(eng, s):
            n = [0]

            def link(ins):
                n[0] += 1
                ins.then_inc(s, 1)
                eng.wait_ge(s, n[0])
            return link

        def bc(ap, shape):
            return ap.unsqueeze(len(ap.shape)).to_broadcast(shape)

        def bc1(ap, shape):
            return ap.unsqueeze(1).to_broadcast(shape)

        def slot_of(m):
            return m + 2 if m < NC else m - NC

        def latents_of(m):
            return cached[:, m] if m < NC else cn[m % 2]

        def ahead(eng, value):
            return value if isinstance(value, int) else eng.snap(value)

        def load_x(eng, n, s, j):
            row = ahead(eng, n * P)
            eng.wait_ge(xt_full[s], j + 1)
            eng.wait_ge(x_ssq[s], j + 1)
            eng.dma_start(xin[s], T["x_rows"][bass.ds(row, P), :]).then_inc(x_in[s], 16)

        def store_z(eng, n, s):
            row, count = ahead(eng, n * P), ahead(eng, n + 1)
            for c in range(4):
                eng.wait_ge(z_read[c], count)
            eng.dma_start(z_dram[bass.ds(row, P), :], zst[s]).then_inc(zst_out[s], 16)

        def load_expert(eng, e, s, signals, done=None):
            row_up, row_down = ahead(eng, e * D), ahead(eng, e * FF)
            count = None if done is None else ahead(eng, done)
            for row, dst, src, signal, used in ((row_up, w1s[s], "w1", signals[0], h1_full),
                                                (row_up, w3s[s], "w3", signals[1], h3_full),
                                                (row_down, w2s[s], "w2", signals[2], y_full)):
                if done is not None:
                    eng.wait_ge(used, count)
                load_part(eng, row, dst, src, signal)

        def load_part(eng, row, dst, src, signal):
            rows = T[src].rearrange("e a n -> (e a) n")[bass.ds(row, T[src].shape[1]), :]
            eng.dma_start(dst, rows.rearrange("(k p) n -> p k n", p=P)).then_inc(signal, 16)

        def gate_col(b):
            return slot_gate[:, bass.ds(b, 1)]

        def take_pT(copy, o, part, at, q, key):
            whole = [p for p in part if p[3] == P]
            ins = None
            if whole:
                k = len(whole)
                src = o[:, 0:k * P].rearrange("p (a b) -> p a b", b=P)
                ins = copy(pT[:, at:at + k, 0:q], src[:, :, 0:q])
            if len(whole) < len(part):
                k, w = len(whole), part[-1][3]
                ins = copy(pT[0:w, at + k, 0:q], o[0:w, k * P:k * P + q])
            done_read(ins, key)

        def wait_values(eng, n, h):
            if (n, h) != (0, 0):
                eng.wait_ge(pv_done, n * HA + h)

        @block.sync
        def _(sp_):
            sp_.dma_start(ident[:], T["ident"]).then_inc(const_in, 16)
            sp_.dma_start(w_ukv, T["w_ukv"]).then_inc(kvw_in, 16)
            sp_.dma_start(cached[:, :, 0:KL], T["cache_ckv"].rearrange("(c p) k -> p c k", p=P)).then_inc(cache_in, 16)
            sp_.dma_start(cached[:, :, KL:], T["cache_kr"].rearrange("(c p) k -> p c k", p=P)).then_inc(cache_in, 16)
            sp_.dma_start(g_attn, T["g_attn"]).then_inc(const_in, 16)
            for s in range(2):
                sp_.dma_start(xin[s], T["x_rows"][s * P:(s + 1) * P, :]).then_inc(x_in[s], 16)
            sp_.dma_start(w_in, T["w_in"].rearrange("(k p) n -> p k n", p=P)).then_inc(win_in, 16)
            sp_.dma_start(before[:], T["before"]).then_inc(mixw_in, 16)
            sp_.dma_start(route_rows[:], T["route_rows"]).then_inc(mixw_in, 16)
            for dst, src in ((g_cq, "g_cq"), (g_qk[:, 0:1], "g_q"), (g_qk[:, 1:2], "g_k"), (b_gate, "b_gate"),
                             (mstate, "state_m")):
                sp_.dma_start(dst, T[src]).then_inc(mixw_in, 16)
            sp_.dma_start(b_route, T["b_route"].to_broadcast([P, NG + NE])).then_inc(mixw_in, 16)
            sp_.dma_start(rope, T["rope"].rearrange("p (n a r) -> p n a r", n=NT, a=2)).then_inc(mixw_in, 16)
            sp_.dma_start(pick, T["pick_head"].rearrange("p (a b) -> p a b", b=P)).then_inc(mixw_in, 16)
            with sp_.Fori(0, NT // 2 - 1) as j:
                for s in range(2):
                    load_x(sp_, 2 * j + s + 2, s, j)
                    store_z(sp_, 2 * j + s, s)
            load_x(sp_, NT - 1, 0, NT // 2 - 1)
            for n in range(NT - 3, NT):
                store_z(sp_, n, n % 2)
            for s in range(2):
                sp_.wait_ge(zst_out[s], 16 * (NT // 2 + (s == 0)))
            for i in range(4):
                sp_.wait_ge(z_full[i], NT)
            sp_.dma_start(gate_rows, T["gate_rows"].rearrange("p (a b) -> p a b", b=ROWS)).then_inc(gate_in, 16)
            sp_.dma_start(z_lat, z_dram[0:P, 0:Z_MQ]).then_inc(zl_in, 16)
            sp_.dma_start(w_uq, T["w_uq"].rearrange("(k p) n -> p k n", p=P)).then_inc(wuq_in, 16)
            sp_.dma_start(g_ckv, T["g_ckv"].to_broadcast([P, KL])).then_inc(wuq_in, 16)
            sp_.dma_start(z_rec, z_dram[0:P, Z_MQ:]).then_inc(zr_in, 16)
            sp_.dma_start(w_out, T["w_out"].rearrange("(k p) n -> p k n", p=P)).then_inc(wout_in, 16)
            sp_.dma_start(w_route, T["w_route"].rearrange("(k p) n -> p k n", p=P)).then_inc(wout_in, 16)
            for n in range(-1, NT + 1):
                if n >= 1:
                    if n >= 2:
                        sp_.wait_ge(x1_out, 16 * (n - 1))
                        sp_.wait_ge(xn_ok, n - 1)
                    sp_.dma_start(xres, T["x_rows"][(n - 1) * P:n * P, :]).then_inc(xres_in, 16)
                if n + 1 < NT:
                    r = slice((n + 1) * P, (n + 2) * P)
                    src = cn[(NC + n + 1) % 2]
                    sp_.wait_ge(cn_ok, n + 2)
                    sp_.dma_start(O["ckv"][r, :], src[:, 0:KL]).then_inc(kv_out[(n + 1) % 2], 16)
                    sp_.dma_start(O["krope"][r, :], src[:, KL:]).then_inc(kv_out[(n + 1) % 2], 16)
                if n + 2 < NT:
                    sp_.wait_ge(in_ssq, 2 * (n + 2))
                    wait_full(sp_, ("cqT", n + 1))
                    sp_.dma_start(z_lat, z_dram[(n + 2) * P:(n + 3) * P, 0:Z_MQ]).then_inc(zl_in, 16)
                if n == -1:
                    wait_read(sp_, ("v", NC))
                    sp_.dma_start(Vmeta, V[DEC:DEC + META, 0, :]).then_inc(vmeta_in, 16)
                    sp_.wait_ge(g_ok, 3)
                    sp_.dma_start(chunk_mask, T["chunk_mask"]).then_inc(wout_in, 16)
                    sp_.dma_start(g_mh, T["g_mh"].to_broadcast([P, HM * DV])).then_inc(wout_in, 16)
                    sp_.dma_start(g_ffn, T["g_ffn"].to_broadcast([P, D])).then_inc(wout_in, 16)
                    sp_.wait_ge(zero_ok, 5)
                    sp_.dma_start(state[0][0:DK], T["state_c"].rearrange("p (a b) -> p a b", b=CAUG)).then_inc(wout_in, 16)
                    for col, c in ((0, NCH - 1), (1, 0)):
                        sp_.dma_start(O["m_both"][col], m_out[:, c:c + 1]).then_inc(m_store, 16)
                if n == 0:
                    sp_.wait_ge(st1_ok, HM)
                    sp_.dma_start(O["c_sample"], state[1][DK:P].rearrange("p a b -> p (a b)")).then_inc(state_out, 16)
                if n >= 1:
                    r = slice((n - 1) * P, n * P)
                    wait_read(sp_, ("o1", n - 1))
                    sp_.dma_start(O["y"][r, :], xres).then_inc(x1_out, 16)
                    sp_.wait_ge(xn_ok, n)
                    sp_.dma_start(xn_dram[r, :], xn).then_inc(xn_out, 16)
                if 0 <= n and n + 1 < NT:
                    sp_.wait_ge(packed, 5 * (n + 1))
                    sp_.wait_ge(og_ok, n + 1)
                    sp_.dma_start(z_rec, z_dram[(n + 1) * P:(n + 2) * P, Z_MQ:]).then_inc(zr_in, 16)
            wait_read(sp_, ("ub", NT - 1))
            sp_.dma_start(O["c_prompt"], state[NT % 2][0:DK].rearrange("p a b -> p (a b)")).then_inc(state_out, 16)
            sp_.wait_ge(state_out, 32)
            sp_.wait_ge(m_store, 32)
            sp_.wait_ge(kv_out[0], 32 * ((NT + 1) // 2))
            sp_.wait_ge(kv_out[1], 32 * (NT // 2))
            sp_.wait_ge(x1_out, 16 * NT)
            sp_.wait_ge(xn_out, 16 * NT)
            wait_read(sp_, ("lg", NT - 1))
            load_expert(sp_, 0, 0, (w1_in[0], w3_in[0], w2_in[0]))
            load_part(sp_, D, w1s[1], "w1", w1_in[1])
            for s in range(2):
                sp_.wait_ge(xe_in[s], 16)
            load_part(sp_, D, w3s[1], "w3", w3_in[1])
            load_part(sp_, FF, w2s[1], "w2", w2_in[1])
            with sp_.Fori(0, NE // 2 - 1) as j:
                for s in range(2):
                    load_expert(sp_, 2 * j + s + 2, s, (w1_in[s], w3_in[s], w2_in[s]), 2 * j + s + 1)
            sp_.wait_ge(y_full, NE)
            total = sp_.value_load(over_e[0:1, MAX_OVER:MAX_OVER + 1], min_val=0, max_val=MAX_OVER)
            with sp_.If(total > 0):
                with sp_.Fori(0, MAX_OVER) as j:
                    with sp_.If(j < total):
                        e = sp_.value_load(over_e[0:1, bass.ds(j, 1)], min_val=0, max_val=NE - 1)
                        load_expert(sp_, e, 0, (ov_w, ov_w, ov_w), NE + j)
        @block.tensor
        def _(pe):
            order = sorted(fills, key=lambda k: (fills[k][1] * 4 + fills[k][0]))
            at = [0]

            def open_bank(key):
                assert order[at[0]] == key, (order[at[0]], key)
                at[0] += 1
                b, k = fills[key]
                if k:
                    pe.wait_ge(read[b], k)
                return bank(RB[b])

            def filled(ins, key):
                ins.then_inc(full[fills[key][0]], 1)

            def transposes(key, parts, width, sources):
                o = open_bank(key)
                for i, src in enumerate(sources):
                    rows = src.shape[0]
                    ins = pe.transpose(o[0:width, i * P:i * P + rows], src, ident[0:rows, 0:rows])
                filled(ins, key)

            def key_values(m, what):
                if what == "ckvT":
                    if m < NC:
                        pe.wait_ge(cache_in, 32)
                    else:
                        pe.wait_ge(cn_ok, m - NC + 1)
                    transposes(("ckvT", m), P, KL, [latents_of(m)[:, 0:KL]])
                if what in ("kn", "v"):
                    wait_read(pe, ("ckvT", m))
                    off = 0 if what == "kn" else HA * NOPE
                    o = open_bank((what, m))
                    filled(pe.matmul(o, ckvT[m % 2], w_ukv[:, off:off + BANK], start=True, stop=True), (what, m))
                if what in ("kTa", "kTb"):
                    pe.wait_ge(kk_ok, m + 1)
                    h0 = 0 if what == "kTa" else 4
                    transposes((what, m), P, QK, [kk[m % 2][:, h, :] for h in range(h0, h0 + 4)])

            pe.wait_ge(const_in, 16)
            pe.wait_ge(kvw_in, 16)
            for c in range(NC + 2):
                for what, m in cache_step(c):
                    key_values(m, what)
            for b in range(4):
                pe.wait_ge(read[b], [sum(1 for k in order[:at[0]] if fills[k][0] == i) for i in range(4)][b])

            def x_transposes(s, j):
                pe.wait_ge(x_in[s], 16 * (j + 1))
                pe.wait_ge(xt_read[s], j)
                o = bank(2 * s, 2)
                for k in range(KD):
                    ins = pe.transpose(o[:, k * P:(k + 1) * P], xin[s][:, k * P:(k + 1) * P], ident[:])
                ins.then_inc(xt_full[s], 1)

            def x_gemm(s, n, j):
                pe.wait_ge(xt_read[s], j + 1)
                for c, (lo, hi) in enumerate(Z_CHUNKS):
                    pe.wait_ge(z_read[c], n)
                    o = bank(4 + c)
                    for k in range(KD):
                        ins = pe.matmul(o[:, 0:hi - lo], xT[s][:, k, :], w_in[:, k, lo:hi],
                                        start=(k == 0), stop=(k == KD - 1))
                    ins.then_inc(z_full[c], 1)

            x_transposes(0, 0)
            pe.wait_ge(win_in, 16)
            with pe.Fori(0, NT // 2) as j:
                x_transposes(1, j)
                x_gemm(0, 2 * j, j)
                x_transposes(0, j + 1)
                x_gemm(1, 2 * j + 1, j)
            x_gemm(0, NT - 1, NT // 2)
            for c in range(4):
                pe.wait_ge(z_read[c], NT)

            for g in range(2):
                if g:
                    pe.wait_ge(s_read, 1)
                o = bank(0, 3)
                for n in range(NT):
                    ins = pe.transpose(o[0:HM, n * P:(n + 1) * P], gat[:, n, g * HM:(g + 1) * HM], ident[:])
                ins.then_inc(s_full, 1)

            def step(key):
                what, n = key
                if what in NO_BANK:
                    return
                if what in ("ckvT", "kn", "v", "kTa", "kTb"):
                    key_values(n, what)
                elif what == "cqT":
                    pe.wait_ge(zl_in, 16 * (n + 1))
                    transposes(key, P, P, [z_lat[:, Z_CQ + i * P:Z_CQ + (i + 1) * P] for i in range(2)])
                elif what in ("q0", "q1"):
                    wait_read(pe, ("cqT", n))
                    o = open_bank(key)
                    w = HA * QK // 2
                    lo = 0 if what == "q0" else w
                    for k in range(2):
                        ins = pe.matmul(o[:, 0:w], cqT[:, k, :], w_uq[:, k, lo:lo + w], start=(k == 0), stop=(k == 1))
                    filled(ins, key)
                elif what in ("qTa", "qTb"):
                    pe.wait_ge(q_ok, n + 1)
                    h0 = 0 if what == "qTa" else 4
                    transposes(key, P, QK, [qk[:, h, :] for h in range(h0, h0 + 4)])
                elif what == "gt":
                    pe.wait_ge(g_ok, 3)
                    transposes(key, P, P, [GQ[:, n * P:(n + 1) * P]])
                elif what == "nm":
                    o = open_bank(key)
                    for h in range(HM):
                        ins = pe.matmul(o[:, h * P:(h + 1) * P], pick[:, h, :], NM[:, n * P:(n + 1) * P],
                                        start=True, stop=True)
                    filled(ins, key)
                elif what in ("qbT", "kbT"):
                    pe.wait_ge(packed, 5 * (n + 1))
                    src = qb if what == "qbT" else kb
                    transposes(key, P, P, [src[:, h, :] for h in range(HM)])
                elif what == "qkm":
                    wait_read(pe, ("qbT", n))
                    wait_read(pe, ("kbT", n))
                    o = open_bank(key)
                    for h in range(HM):
                        ins = pe.matmul(o[:, h * P:(h + 1) * P], kbT[:, h, :], qbT[:, h, :], start=True, stop=True)
                    filled(ins, key)
                elif what in ("ua", "ub", "ia", "ib", "na", "nb"):
                    lhs, rhs = {"u": (kw, vaug), "i": (qbT, state[n % 2]), "n": (Dm, vaug)}[what[0]]
                    if what == "ua":
                        pe.wait_ge(kw_ok, n + 1)
                    if what == "ia":
                        pe.wait_ge(st1_ok, 4 * (n + 1))
                        if n:
                            wait_read(pe, ("ub", n - 1))
                    if what == "na":
                        wait_read(pe, ("qkm", n))
                    o = open_bank(key)
                    h0 = 0 if what[1] == "a" else 2
                    for h in range(h0, h0 + 2):
                        ins = pe.matmul(o[:, (h - h0) * CAUG:(h - h0 + 1) * CAUG], lhs[:, h, :], rhs[:, h, :],
                                        start=True, stop=True)
                    filled(ins, key)
                elif what in ("mxa", "mxb"):
                    pe.wait_ge(mm_ok, n + 1)
                    pe.wait_ge(o_read, n + 1)
                    k0 = 0 if what == "mxa" else 4
                    transposes(key, P, P, [mix[:, k * P:(k + 1) * P] for k in range(k0, k0 + 4)])
                elif what in ("o0", "o1"):
                    wait_read(pe, ("mxa", n))
                    wait_read(pe, ("mxb", n))
                    o = open_bank(key)
                    lo = 0 if what == "o0" else BANK
                    for k in range(KD):
                        ins = pe.matmul(o, mixT[:, k, :], w_out[:, k, lo:lo + BANK], start=(k == 0), stop=(k == KD - 1))
                    filled(ins, key)
                elif what in ("xna", "xnb"):
                    pe.wait_ge(xn_ok, n + 1)
                    k0 = 0 if what == "xna" else 4
                    transposes(key, P, P, [xn[:, k * P:(k + 1) * P] for k in range(k0, k0 + 4)])
                elif what == "lg":
                    wait_read(pe, ("xna", n))
                    wait_read(pe, ("xnb", n))
                    o = open_bank(key)
                    for k in range(KD):
                        ins = pe.matmul(o[:, 0:NG + NE], xnT[:, k, :], w_route[:, k, :], start=(k == 0), stop=(k == KD - 1))
                    filled(ins, key)
                else:
                    raise AssertionError(what)

            def scores(n, h):
                pe.wait_ge(s_read, 3 + n * HA + h)
                if h == 0:
                    wait_read(pe, ("qTa", n))
                    wait_read(pe, ("kTa", NC + n))
                    wait_read(pe, ("kTb", NC + n))
                if h == 4:
                    wait_read(pe, ("qTb", n))
                q = DEC if n == 0 else P
                blocks = key_blocks(n)
                o = bank(0, 3)
                last = blocks[-1]
                runs = [(i, min(i + BANK, last[0])) for i in range(0, last[0], BANK)]
                for lo, hi in runs:
                    k0 = blocks[0][1] * P + lo
                    pe.matmul(o[0:q, lo:hi], qT[n % 2][:, h, 0:q], KT[:, h, k0:k0 + hi - lo], start=True, stop=True)
                lo, _, k0, w = last
                pe.matmul(o[0:q, lo:lo + w], qT[n % 2][:, h, 0:q], KT[:, h, k0:k0 + w],
                          start=True, stop=True).then_inc(s_full, 1)

            def probs_transposes(n, h):
                pe.wait_ge(s_read, 3 + n * HA + h + 1)
                q = DEC if n == 0 else P
                blocks = key_blocks(n)
                for g in range((len(blocks) + 3) // 4):
                    key = ("pT", n, h, g)
                    o = open_bank(key)
                    for i, (lo, _, _, w) in enumerate(blocks[4 * g:4 * g + 4]):
                        ins = pe.transpose(o[0:w, i * P:i * P + q], probs[0:q, lo:lo + w], ident[0:q, 0:q])
                    filled(ins, key)

            def values(n, h):
                q = DEC if n == 0 else P
                blocks = key_blocks(n)
                for g in range((len(blocks) + 3) // 4):
                    wait_read(pe, ("pT", n, h, g))
                if h == 0:
                    wait_read(pe, ("v", NC + n))
                    pe.wait_ge(vmeta_in, 16)
                    if n:
                        pe.wait_ge(o_read, n)
                o = bank(4)[0:q, h * VD:(h + 1) * VD]
                for i, (_, slot, k0, w) in enumerate(blocks):
                    v = Vmeta[:, h * VD:(h + 1) * VD] if k0 else V[0:w, slot, h * VD:(h + 1) * VD]
                    ins = pe.matmul(o, pT[0:w, i, 0:q], v, start=(i == 0), stop=(i == len(blocks) - 1))
                ins.then_inc(pv_done, 1)

            def chunk_decays():
                pe.wait_ge(g_ok, 1)
                pe.wait_ge(mixw_in, 16 * 10)
                pe.wait_ge(s_read, 2)
                for h in range(HM):
                    ins = pe.matmul(bank(0)[:, h * NCH:(h + 1) * NCH], pick[:, h, :], dec4, start=True, stop=True)
                ins.then_inc(s_full, 1)
                pe.wait_ge(s_read, 3)

            pe.wait_ge(wuq_in, 32)
            for n in range(-1, NT + 1):
                now = 0 <= n < NT
                if n == 0:
                    chunk_decays()
                if now:
                    scores(n, 0)
                for h in range(HA):
                    if (n, h) == (0, 1):
                        pe.wait_ge(wout_in, 16 * 6)
                    for key in filler(n, h):
                        step(key)
                    if now:
                        if h:
                            values(n, h - 1)
                        probs_transposes(n, h)
                        if h + 1 < HA:
                            scores(n, h + 1)
                for key in filler(n, HA):
                    step(key)
                if now:
                    values(n, HA - 1)
            assert at[0] == len(order)

            for b in range(4):
                pe.wait_ge(read[b], ring_used[b])
            pe.wait_ge(r_dve, 1)
            pe.wait_ge(ones_ok, 1)
            w = NT * NE
            pe.matmul(bank(0)[:, 0:w], before[:], rt["m"].rearrange("p a b -> p (a b)"), start=True, stop=False)
            pe.matmul(bank(0)[:, 0:w], ones[:], rt["mp"][:, 0:NT].rearrange("p a b -> p (a b)"), start=False, stop=True)
            pe.matmul(bank(1)[:, 0:NE], ones[:], rt["mp"][:, NT], start=True, stop=True).then_inc(r_pe, 1)
            for k in range(2):
                pe.wait_ge(hot_ok, k + 1)
                for i in range(k * NT, (k + 1) * NT):
                    ins = pe.matmul(bank(2)[:, 0:3 * NBLK], rt["rows"][:, i], rt["blocks"][:, i],
                                    start=(i == 0), stop=(i == 2 * NT - 1))
            ins.then_inc(r_pe, 1)
            pe.wait_ge(tab_ok, 1)

            def gather_transposes(s, b, arrived, count):
                pe.wait_ge(arrived, count)
                pe.wait_ge(xeT_read, b)
                for k in range(KD):
                    ins = pe.transpose(bank(0, 2)[:, k * P:(k + 1) * P], xe[s][:, k * P:(k + 1) * P], ident[:])
                ins.then_inc(xeT_full, 1)

            def hidden_1(s, b, arrived, count, between=None):
                pe.wait_ge(arrived, count)
                pe.wait_ge(xeT_read, b + 1)
                pe.wait_ge(u_ok, b)
                for k in range(KD):
                    if k == KD // 2 and between is not None:
                        between()
                    ins = pe.matmul(bank(2), xeT[s][:, k, :], w1s[s][:, k, :], start=(k == 0), stop=(k == KD - 1))
                ins.then_inc(h1_full, 1)

            def hidden_3(s, b, arrived, count):
                pe.wait_ge(arrived, count)
                pe.wait_ge(hh_ok, b)
                for k in range(KD):
                    ins = pe.matmul(bank(3), xeT[s][:, k, :], w3s[s][:, k, :], start=(k == 0), stop=(k == KD - 1))
                ins.then_inc(h3_full, 1)

            def hidden_transposes(b):
                pe.wait_ge(hh_ok, b + 1)
                pe.wait_ge(hT_read, b)
                for k in range(KF):
                    ins = pe.transpose(bank(4)[:, k * P:(k + 1) * P], hh[:, k * P:(k + 1) * P], ident[:])
                ins.then_inc(hT_full, 1)

            def down(s, b, arrived, count):
                pe.wait_ge(arrived, count)
                pe.wait_ge(hT_read, b + 1)
                pe.wait_ge(y_read, b)
                for c in range(2):
                    for k in range(KF):
                        ins = pe.matmul(bank(5 + c), hT[:, k, :], w2s[s][:, k, c * BANK:(c + 1) * BANK],
                                        start=(k == 0), stop=(k == KF - 1))
                ins.then_inc(y_full, 1)

            gather_transposes(0, 0, xe_in[0], 16)
            hidden_1(0, 0, w1_in[0], 16)
            gather_transposes(1, 1, xe_in[1], 16)
            hidden_3(0, 0, w3_in[0], 16)
            with pe.Fori(0, NE // 2 - 1) as j:
                for i in range(2):
                    b, s = 2 * j + 1 + i, 1 - i
                    now, last = 16 * j + 16 * (1 + i), 16 * j + 16
                    hidden_1(s, b, w1_in[s], now, lambda: hidden_transposes(b - 1))
                    down(1 - s, b - 1, w2_in[1 - s], last)
                    gather_transposes(1 - s, b + 1, xe_in[1 - s], 16 * j + 32)
                    hidden_3(s, b, w3_in[s], now)
            hidden_1(1, NE - 1, w1_in[1], 16 * (NE // 2), lambda: hidden_transposes(NE - 2))
            down(0, NE - 2, w2_in[0], 16 * (NE // 2))
            hidden_3(1, NE - 1, w3_in[1], 16 * (NE // 2))
            hidden_transposes(NE - 1)
            down(1, NE - 1, w2_in[1], 16 * (NE // 2))
            total = pe.value_load(over_e[0:1, MAX_OVER:MAX_OVER + 1], min_val=0, max_val=MAX_OVER)
            with pe.If(total > 0):
                with pe.Fori(0, MAX_OVER) as j:
                    with pe.If(j < total):
                        gather_transposes(0, NE + j, ov_xe, 16 * j + 16)
                        hidden_1(0, NE + j, ov_w, 48 * j + 48)
                        hidden_3(0, NE + j, ov_w, 48 * j + 48)
                        hidden_transposes(NE + j)
                        down(0, NE + j, ov_w, 48 * j + 48)

        @block.scalar
        def _(act):
            link = chain(act, act_link)

            def kv_squares(m):
                if m < NC:
                    act.wait_ge(cache_in, 32)
                else:
                    act.wait_ge(cn_ok, m - NC + 1)
                if m >= 2:
                    act.wait_ge(kv_stats, m - 1)
                act.wait_ge(kr_ssq, m)
                if m > NC:
                    act.wait_ge(in_ssq, 2 * (m - NC + 1))
                act.activation(kjunk[:, 0:ROPE], latents_of(m)[:, KL:], ACT.Square, accum_out=krss[m % 2]).then_inc(kr_ssq, 1)

            def kv_latent(m):
                o = wait_full(act, ("ckvT", m))
                if m >= 2:
                    wait_full(act, ("v", m - 2))
                done_read(act.activation(ckvT[m % 2], o[:, 0:P], ACT.Copy), ("ckvT", m))

            def kv_products(m):
                o = wait_full(act, ("kn", m))
                if m:
                    act.wait_ge(kv_stats, m)
                act.activation(sqk, o, ACT.Square).then_inc(kn_sq, 1)
                if m >= 2:
                    wait_full(act, ("kTb", m - 2))
                done_read(act.activation(kk[m % 2][:, :, 0:NOPE], o.rearrange("p (h d) -> p h d", d=NOPE), ACT.Copy),
                          ("kn", m))
                o = wait_full(act, ("v", m))
                n = m - NC
                if n >= 2:
                    act.wait_ge(pv_done, HA)
                done_read(act.activation(V[:, slot_of(m), :], o, ACT.Copy), ("v", m))

            def kT_take(m, what):
                o = wait_full(act, (what, m))
                n = m - NC
                if n >= 2:
                    act.wait_ge(pv_done, HA)
                h0 = 0 if what == "kTa" else 4
                at = slot_of(m) * P
                done_read(act.activation(KT[:, h0:h0 + 4, at:at + P],
                                         o[0:QK].rearrange("p (a b) -> p a b", b=P), ACT.Copy), (what, m))

            for c in range(NC + 2):
                for what, m in cache_step(c):
                    if what == "ckvT":
                        kv_squares(m)
                        kv_latent(m)
                    elif what == "kn":
                        kv_products(m)
                    elif what != "v":
                        kT_take(m, what)

            def x_squares(s, j):
                act.wait_ge(x_in[s], 16 * (j + 1))
                act.wait_ge(x_ssq[1 - s], j + s)
                act.activation(junk, xin[s], ACT.Square, scale=1.0 / 32, accum_out=xss[s]).then_inc(x_ssq[s], 1)

            def z_take(s, n, j):
                act.wait_ge(x_rstd[s], j + 1)
                act.wait_ge(zst_out[s], 16 * j)
                for c in (0, 2):
                    lo, hi = Z_CHUNKS[c]
                    act.wait_ge(z_full[c], n + 1)
                    if c == 0:
                        act.activation(gat[:, bass.ds(n, 1), :].rearrange("p a b -> p (a b)"),
                                       bank(4)[:, Z_GATE:Z_GATE + 2 * HM], ACT.Copy, scale=xrs[s])
                    act.activation(zst[s][:, lo:hi], bank(4 + c)[:, 0:hi - lo], ACT.Copy,
                                   scale=xrs[s]).then_inc(z_read[c], 1)

            x_squares(0, 0)
            with act.Fori(0, NT // 2) as j:
                x_squares(1, j)
                z_take(0, 2 * j, j)
                x_squares(0, j + 1)
                z_take(1, 2 * j + 1, j)
            z_take(0, NT - 1, NT // 2)

            def gate_logs():
                act.wait_ge(s_read, 2)
                link(act.activation(gA, gF, ACT.Abs))
                link(act.activation(gA, gA, ACT.Exp, scale=-1.0))
                act.activation(gA, gA, ACT.Ln, bias=1.0).then_inc(g_a, 1)

            def fill_work(key):
                what, n = key
                if what == "cqT":
                    act.wait_ge(zl_in, 16 * (n + 1))
                    if n:
                        act.wait_ge(in_rstd, n)
                    z = z_lat
                    act.activation(sqq.rearrange("p a b -> p (a b)")[:, 0:QL], z[:, Z_CQ:Z_CQ + QL], ACT.Square,
                                   scale=QL ** -0.5, accum_out=st_in[:, 0:1]).then_inc(in_ssq, 1)
                    act.wait_ge(kr_ssq, NC + n)
                    act.activation(kjunk, z[:, Z_CKV:Z_CKV + KL], ACT.Square,
                                   scale=KL ** -0.5, accum_out=st_in[:, 1:2]).then_inc(in_ssq, 1)
                elif what == "ckvT":
                    kv_squares(n)
                    kv_latent(n)
                elif what in ("q0", "q1"):
                    w = HA * QK // 2
                    lo = 0 if what == "q0" else w
                    o = wait_full(act, key)
                    act.wait_ge(in_rstd, n + 1)
                    if n and what == "q0":
                        wait_full(act, ("qTb", n - 1))
                    dst = qk.rearrange("p a b -> p (a b)")[:, lo:lo + w]
                    done_read(act.activation(dst, o[:, 0:w], ACT.Copy, scale=rs_in[:, 0:1]), key)
                    if what == "q1":
                        wait_read(act, ("q0", n))
                        wait_read(act, ("q1", n))
                        act.activation(sqq, qk, ACT.Square).then_inc(q_sq, 1)
                elif what == "kn":
                    kv_products(n)
                elif what == "v":
                    pass
                elif what in ("kTa", "kTb"):
                    kT_take(n, what)
                elif what in ("qTa", "qTb"):
                    o = wait_full(act, key)
                    h0 = 0 if what == "qTa" else 4
                    done_read(act.activation(qT[n % 2][:, h0:h0 + 4, :], o[0:QK].rearrange("p (a b) -> p a b", b=P),
                                             ACT.Copy, scale=g_qk[:, 2:3]), key)
                elif what == "gt":
                    o = wait_full(act, key)
                    if n:
                        act.wait_ge(h_ok, n)
                        act.wait_ge(kw_ok, n)
                    done_read(act.activation(gt, o[:, 0:P], ACT.Copy), key)
                elif what == "nm":
                    act.wait_ge(zr_in, 16 * (n + 1))
                    if n:
                        act.wait_ge(mm_ok, n)
                    act.activation(og, z_rec[:, Z_MO - Z_MQ:], ACT.Tanh, scale=0.5).then_inc(og_ok, 1)
                    act.wait_ge(d_ok, n + 1)
                    act.activation(Dm, Dm, ACT.Exp).then_inc(e_ok, 1)
                elif what == "qbT":
                    o = wait_full(act, key)
                    done_read(act.activation(qbT, o.rearrange("p (a b) -> p a b", b=P), ACT.Copy), key)
                elif what == "hsq":
                    act.wait_ge(h_ok, n + 1)
                    act.activation(Dm, hm, ACT.Square).then_inc(hsq_ok, 1)
                elif what == "mxa":
                    o = wait_full(act, key)
                    if n:
                        wait_full(act, ("lg", n - 1))
                    done_read(act.activation(mixT[:, 0:4], o.rearrange("p (a b) -> p a b", b=P), ACT.Copy), key)
                elif what == "o1":
                    wait_read(act, ("o1", n))
                    if n:
                        act.wait_ge(xn_out, 16 * n)
                        wait_full(act, ("xnb", n - 1))
                    act.activation(xn, xres, ACT.Square, scale=1.0 / 32, accum_out=st_x).then_inc(x1_sq, 1)
                elif what == "xna":
                    o = wait_full(act, key)
                    wait_full(act, ("o1", n))
                    done_read(act.activation(xnT[:, 0:4], o.rearrange("p (a b) -> p a b", b=P), ACT.Copy), key)

            def exps(n, h):
                q = DEC if n == 0 else P
                last = key_blocks(n)[-1]
                w = last[0] + last[3]
                act.wait_ge(max_ok, n * HA + h + 1)
                if n or h:
                    pn, ph = (n, h - 1) if h else (n - 1, HA - 1)
                    g = (len(key_blocks(pn)) + 3) // 4 - 1
                    wait_full(act, ("pT", pn, ph, g))
                if h == 0 and n:
                    act.wait_ge(o_read, n)
                act.activation(probs[0:q, 0:w], bank(0, 3)[0:q, 0:w], ACT.Exp, bias=nmax[0:q, h:h + 1],
                               accum_out=rsum[0:q, h:h + 1]).then_inc(s_read, 1)

            def pT_take(n, h):
                q = DEC if n == 0 else P
                blocks = key_blocks(n)
                for g in range(1, (len(blocks) + 3) // 4, 2):
                    part = blocks[4 * g:4 * g + 4]
                    key = ("pT", n, h, g)
                    o = wait_full(act, key)
                    wait_values(act, n, h)
                    take_pT(lambda d, s: act.activation(d, s, ACT.Copy), o, part, 4 * g, q, key)

            def gate_exps():
                act.wait_ge(g_v, 1)
                act.activation(dec4, dec4, ACT.Exp).then_inc(g_ok, 1)
                for rows in (GQ[32:64], GQ[64:128]):
                    act.activation(rows, rows, ACT.Exp).then_inc(g_ok, 1)
                act.wait_ge(s_read, 3)

            act.wait_ge(wuq_in, 32)
            act.wait_ge(g_qk_ok, 1)
            act.wait_ge(mixw_in, 16 * 10)
            for n in range(-1, NT + 1):
                now = 0 <= n < NT
                if n == 0:
                    gate_exps()
                if now:
                    exps(n, 0)
                for h in range(HA):
                    if (n, h) == (-1, 2):
                        gate_logs()
                    if (n, h) == (0, 1):
                        act.wait_ge(wout_in, 16 * 6)
                    for key in filler(n, h):
                        fill_work(key)
                    if now:
                        pT_take(n, h)
                        if h + 1 < HA:
                            exps(n, h + 1)
                for key in filler(n, HA):
                    fill_work(key)

            act.wait_ge(r_dve, 1)
            act.activation(rt["ge"], rt["ge"], ACT.Exp).then_inc(r_act, 1)
            act.activation(rt["cols"][:, 6], rt["cols"][:, 6], ACT.Exp).then_inc(r_act, 1)

            def silu_tanh(b):
                act.wait_ge(h1_full, b + 1)
                act.wait_ge(u_ok, b)
                act.activation(th, bank(2), ACT.Tanh, scale=0.5).then_inc(tanh_ok, 1)

            def y_take(s, b, col, out_sem, count):
                act.wait_ge(y_full, b + 1)
                act.wait_ge(out_sem, count)
                act.activation(ye[s], bank(5, 2), ACT.Copy, scale=gate_col(col)).then_inc(y_read, 1)

            act.wait_ge(tab_ok, 1)
            silu_tanh(0)
            with act.Fori(0, NE // 2 - 1) as j:
                for s in range(2):
                    b = 2 * j + s
                    silu_tanh(b + 1)
                    y_take(s, b, b, ye_out[s], 16 * j)
            silu_tanh(NE - 1)
            for s in range(2):
                y_take(s, NE - 2 + s, NE - 2 + s, ye_out[s], 16 * (NE // 2 - 1))
            total = act.value_load(over_e[0:1, MAX_OVER:MAX_OVER + 1], min_val=0, max_val=MAX_OVER)
            act.wait_ge(ye_out[0], 16 * (NE // 2))
            with act.If(total > 0):
                with act.Fori(0, MAX_OVER) as j:
                    with act.If(j < total):
                        silu_tanh(NE + j)
                        y_take(0, NE + j, NE + j, ov_ye, 16 * j)

        @block.gpsimd
        def _(pool):
            link = chain(pool, pool_link)
            pool.memset(half, -0.5).then_inc(half_ok, 1)
            pool.wait_ge(half_ok, 1)
            pool.memset(eps, EPS).then_inc(half_ok, 1)
            pool.wait_ge(half_ok, 2)
            pool.memset(ones[:], 1.0).then_inc(ones_ok, 1)
            pool.wait_ge(ones_ok, 1)

            def rsqrt(dst, src, scale, signal, count):
                link(pool.tensor_scalar(dst, src, scale, EPS, ALU.mult, ALU.add))
                n = dst.shape[-1]
                pool.tensor_tensor(dst, dst, half[:, 0:n], ALU.pow).then_inc(signal, 1)
                pool.wait_ge(signal, count)

            def kv_rstd_of(m):
                pool.wait_ge(kv_stats, m + 1)
                part = slice(8, 16) if m < NC else slice(0, 16)
                rsqrt(rs_qk[m % 2][:, part], st_qk[m % 2][:, part], 1.0 / QK, kv_rstd, m + 1)

            for c in range(NC):
                kv_rstd_of(c)
            def row_rstd(s, j, before_it=None):
                pool.wait_ge(x_ssq[s], j + 1)
                if before_it is not None:
                    pool.wait_ge(z_read[2], before_it)
                    pool.wait_ge(z_read[3], before_it)
                pool.tensor_tensor(xrs[s], xss[s], eps, ALU.add).then_inc(rs_mid[s], 1)
                pool.wait_ge(rs_mid[s], j + 1)
                pool.tensor_tensor(xrs[s], xrs[s], half[:, 0:1], ALU.pow).then_inc(x_rstd[s], 1)
                pool.wait_ge(x_rstd[s], j + 1)

            row_rstd(0, 0)
            with pool.Fori(0, NT // 2) as j:
                row_rstd(1, j, 2 * j)
                row_rstd(0, j + 1, 2 * j + 1)
            def clear_mlstm():
                pool.wait_ge(g_ok, 3)
                zero = chain(pool, zero_ok)
                for t in (qb, kb, state[0], state[1]):
                    zero(pool.memset(t, 0.0))
                zero(pool.memset(vaug[:, :, DV:], 1.0))
                pool.wait_ge(wout_in, 16 * 6)

            pack = chain(pool, packed)

            def pool_work(key):
                what, n = key
                if what == "gt":
                    pool.wait_ge(zr_in, 16 * (n + 1))
                    if n:
                        wait_full(pool, ("kbT", n - 1))
                        wait_full(pool, ("nb", n - 1))
                        pool.wait_ge(kw_ok, n)
                    for i in range(2):
                        r = slice(i * CH, (i + 1) * CH)
                        src = z_rec[r, 0:HM * DK].rearrange("p (h d) -> p h d", d=DK)
                        pack(pool.tensor_copy(qb[r, :, i * DK:(i + 1) * DK], src))
                        src = z_rec[r, Z_MK - Z_MQ:Z_MK - Z_MQ + HM * DK].rearrange("p (h d) -> p h d", d=DK)
                        pack(pool.tensor_scalar(kb[r, :, i * DK:(i + 1) * DK], src, DK ** -0.5, 1.0, ALU.mult, ALU.mult))
                    src = z_rec[:, Z_MV - Z_MQ:Z_MO - Z_MQ].rearrange("p (h d) -> p h d", d=DV)
                    pack(pool.tensor_copy(vaug[:, :, 0:DV], src))
                elif what == "cqT":
                    pool.wait_ge(in_ssq, 2 * (n + 1))
                    if n:
                        wait_read(pool, ("q1", n - 1))
                        pool.wait_ge(cn_ok, n)
                    rsqrt(rs_in, st_in, 1.0, in_rstd, n + 1)
                elif what == "ksum":
                    kv_rstd_of(n)
                elif what == "hsq":
                    pool.wait_ge(hs_ok, n + 1)
                    rsqrt(rs_m, st_m, 1.0 / DV, hr_ok, n + 1)
                elif what == "o1":
                    pool.wait_ge(x1_sq, n + 1)
                    rsqrt(rs_x, st_x, 1.0, x1_rs, n + 1)

            pool.wait_ge(wuq_in, 32)
            for n in range(-1, NT + 1):
                if n == 0:
                    clear_mlstm()
                for h in range(HA + 1):
                    for key in filler(n, h):
                        pool_work(key)

            pool.wait_ge(tab_ok, 1)
            pool.wait_ge(xn_out, 16 * NT)

            last_token = pool.to_reg(ROWS - 1)

            def gather(s, b, signal):
                pool.tensor_copy(now_tok[s][:], slot_tok[:, bass.ds(b, 1)]).then_inc(gather_idx, 1)
                pool.wait_ge(gather_idx, b + 1)
                pool.sem_inc(index_steps, 1)
                pool.indirect_dma_start(xe[s], None, xn_dram,
                                        bass.IndirectOffsetOnAxis(ap=now_tok[s][:], axis=0),
                                        bounds_check=last_token, oob_is_err=False).then_inc(signal, 16)

            def scatter(s, b, signal, before, count):
                pool.wait_ge(y_read, b + 1)
                pool.tensor_copy(now_out[s][:], slot_out[:, bass.ds(b, 1)]).then_inc(scatter_idx, 1)
                pool.wait_ge(before, count)
                pool.wait_ge(scatter_idx, b + 1)
                pool.sem_inc(index_steps, 1)
                pool.indirect_dma_start(O["y"], bass.IndirectOffsetOnAxis(ap=now_out[s][:], axis=0),
                                        ye[s], None, bounds_check=last_token, compute_op=ALU.add,
                                        oob_is_err=False).then_inc(signal, 16)

            for s in range(2):
                gather(s, s, xe_in[s])
            with pool.Fori(0, NE // 2 - 1) as j:
                for s in range(2):
                    b = 2 * j + s
                    pool.wait_ge(xeT_full, b + 1)
                    gather(s, b + 2, xe_in[s])
                    scatter(s, b, ye_out[s], ye_out[1 - s], 16 * (j + s))
            for s in range(2):
                scatter(s, NE - 2 + s, ye_out[s], ye_out[1 - s], 16 * (NE // 2 - 1 + s))
            total = pool.value_load(over_e[0:1, MAX_OVER:MAX_OVER + 1], min_val=0, max_val=MAX_OVER)
            pool.wait_ge(ye_out[1], 16 * (NE // 2))
            with pool.If(total > 0):
                with pool.Fori(0, MAX_OVER) as j:
                    with pool.If(j < total):
                        pool.wait_ge(xeT_full, NE + j)
                        gather(0, NE + j, ov_xe)
                        scatter(0, NE + j, ov_ye, ov_ye, 16 * j)
            pool.wait_ge(ye_out[0], 16 * (NE // 2))
            pool.wait_ge(ov_ye, 16 * total)

        @block.vector
        def _(dve):
            link = chain(dve, dve_link)
            TT, TS, STT = dve.tensor_tensor, dve.tensor_scalar, dve.scalar_tensor_tensor

            def kv_sums(m):
                st = st_qk[m % 2]
                dve.wait_ge(kn_sq, m + 1)
                dve.wait_ge(kr_ssq, m + 1)
                if m >= 2:
                    dve.wait_ge(kv_rstd, m - 1)
                link(dve.tensor_reduce(st[:, 8:16], sqk.rearrange("p (h d) -> p h d", d=NOPE), AX, ALU.add))
                TS(st[:, 8:16], st[:, 8:16], krss[m % 2], None, ALU.add).then_inc(kv_stats, 1)

            def kv_norm(m):
                rs = rs_qk[m % 2]
                wait_read(dve, ("kn", m))
                dve.wait_ge(kv_rstd, m + 1)
                if m >= 2:
                    wait_full(dve, ("kTb", m - 2))
                TT(kk[m % 2][:, :, 0:NOPE], kk[m % 2][:, :, 0:NOPE], bc(rs[:, 8:16], [P, HA, NOPE]), ALU.mult)
                TT(kk[m % 2][:, :, NOPE:], bc1(latents_of(m)[:, KL:], [P, HA, ROPE]), bc(rs[:, 8:16], [P, HA, ROPE]),
                   ALU.mult).then_inc(kk_ok, 1)

            for m in range(2):
                dve.memset(st_qk[m], 1.0).then_inc(stq_ok, 1)
            dve.wait_ge(stq_ok, 2)
            for c in range(NC + 1):
                if c < NC:
                    kv_sums(c)
                if c:
                    kv_norm(c - 1)

            def xT_take(s, j, before_it=None):
                dve.wait_ge(xt_full[s], j + 1)
                if before_it is not None:
                    dve.wait_ge(z_full[3], before_it)
                TT(xT[s], bank(2 * s, 2).rearrange("p (k t) -> p k t", t=P), bc(g_attn, [P, KD, P]),
                   ALU.mult).then_inc(xt_read[s], 1)

            def z_take(s, n, j):
                dve.wait_ge(x_rstd[s], j + 1)
                dve.wait_ge(zst_out[s], 16 * j)
                for c in (1, 3):
                    lo, hi = Z_CHUNKS[c]
                    dve.wait_ge(z_full[c], n + 1)
                    TS(zst[s][:, lo:hi], bank(4 + c)[:, 0:hi - lo], xrs[s], None, ALU.mult).then_inc(z_read[c], 1)

            dve.wait_ge(const_in, 32)
            xT_take(0, 0)
            with dve.Fori(0, NT // 2) as j:
                xT_take(1, j, 2 * j)
                z_take(0, 2 * j, j)
                xT_take(0, j + 1, 2 * j + 1)
                z_take(1, 2 * j + 1, j)
            z_take(0, NT - 1, NT // 2)

            keep, negpad, cont, restart = [gate_rows[:, i] for i in range(4)]
            dve.memset(GQ, 0.0).then_inc(gq_zero, 1)
            dve.wait_ge(mixw_in, 16 * 10)
            for s in range(2):
                dve.wait_ge(zst_out[s], 16 * (NT // 2 + (s == 0)))
            dve.wait_ge(s_full, 1)
            TS(gI, bank(0, 3)[0:HM, 0:ROWS], b_gate[:, 0:1], None, ALU.add).then_inc(s_read, 1)
            dve.wait_ge(s_full, 2)
            TS(gF, bank(0, 3)[0:HM, 0:ROWS], b_gate[:, 1:2], None, ALU.add).then_inc(s_read, 1)
            link(TT(g_qk[:, 2:3], g_qk[:, 0:1], g_qk[:, 1:2], ALU.mult))
            TS(g_qk[:, 2:3], g_qk[:, 2:3], QK ** -0.5, None, ALU.mult).then_inc(g_qk_ok, 1)

            by_chunk = lambda a: a.rearrange("p (c t) -> p c t", t=CH)

            def gates_log():
                dve.wait_ge(g_a, 1)
                dve.wait_ge(gate_in, 16)
                link(STT(gF, gF, 0.0, gA, ALU.min, ALU.subtract))
                link(TT(gF[:, 0:P], gF[:, 0:P], keep[:, 0:P], ALU.mult))
                link(dve.tensor_tensor_scan(gB, cont, gF, 0.0, ALU.mult, ALU.add))

            def gates_max():
                link(TT(gI, gI, gB, ALU.subtract))
                link(TT(gI[:, 0:P], gI[:, 0:P], negpad[:, 0:P], ALU.add))
                link(dve.tensor_tensor_scan(gM, restart, gI, 0.0, ALU.add, ALU.max))
                link(dve.tensor_copy(m_last, by_chunk(gM)[:, :, CH - 1]))
                link(dve.tensor_copy(b_last, by_chunk(gB)[:, :, CH - 1]))
                link(dve.tensor_tensor_scan(m_out[:, 1:], m_last[:, 1:], b_last[:, 1:], 0.0, ALU.max, ALU.add))
                link(STT(m_out[:, 0:1], m_last[:, 0:1], mstate, b_last[:, 0:1], ALU.max, ALU.add))
                link(dve.memset(m_prev[:, 1:2], 0.0))
                link(dve.tensor_copy(m_prev[:, 0:1], mstate))
                link(dve.tensor_copy(m_prev[:, 2:], m_out[:, 1:NCH - 1]))

            def gates_rows():
                link(TT(by_chunk(gM), by_chunk(gM), bc(m_prev, [HM, NCH, CH]), ALU.max))
                link(dve.tensor_copy(m_last, by_chunk(gM)[:, :, CH - 1]))
                dve.wait_ge(gq_zero, 1)
                link(dve.tensor_copy(GQ[0:HM], gI))
                link(TT(by_chunk(GQ[32:32 + HM]), bc(m_prev, [HM, NCH, CH]), by_chunk(gM), ALU.subtract))

            def gates_end():
                link(TT(by_chunk(GQ[64:64 + HM]), by_chunk(gI), bc(m_last, [HM, NCH, CH]), ALU.subtract))
                link(TS(NM, gM, -1.0, None, ALU.mult))
                link(TT(GQ[96:96 + HM], NM, gB, ALU.subtract))
                TT(dec4, m_prev, m_last, ALU.subtract).then_inc(g_v, 1)

            def gates_decays():
                dve.wait_ge(s_full, 3)
                dve.tensor_copy(decb, bank(0)[:, 0:HM * NCH]).then_inc(s_read, 1)
                dve.wait_ge(s_read, 3)

            def rotate(x, n, lead, tmp):
                cos, sin = rope[:, n, 0], rope[:, n, 1]
                hr = ROPE // 2
                if lead:
                    cos = bc1(cos, [P, lead, ROPE])
                    s0, s1 = bc1(sin[:, 0:hr], [P, lead, hr]), bc1(sin[:, hr:], [P, lead, hr])
                    lo, hi, tl, th_ = x[:, :, 0:hr], x[:, :, hr:], tmp[:, :, 0:hr], tmp[:, :, hr:]
                else:
                    s0, s1 = sin[:, 0:hr], sin[:, hr:]
                    lo, hi, tl, th_ = x[:, 0:hr], x[:, hr:], tmp[:, 0:hr], tmp[:, hr:]
                link(TT(tl, hi, s0, ALU.mult))
                link(TT(th_, lo, s1, ALU.mult))
                link(TT(x, x, cos, ALU.mult))
                return lambda: TT(x, x, tmp, ALU.add)

            def fill_work(key):
                what, n = key
                if what == "cqT":
                    o = wait_full(dve, key)
                    if n:
                        wait_full(dve, ("q1", n - 1))
                    done_read(TT(cqT, o[:, 0:2 * P].rearrange("p (a b) -> p a b", b=P), bc(g_cq, [P, 2, P]), ALU.mult), key)
                    m = NC + n
                    dve.wait_ge(in_rstd, n + 1)
                    wait_full(dve, ("ckvT", m - 2))
                    dve.wait_ge(kr_ssq, m - 1)
                    if n >= 2:
                        dve.wait_ge(kv_out[n % 2], 32 * (n // 2))
                    z = z_lat
                    link(STT(cn[m % 2][:, 0:KL], z[:, Z_CKV:Z_CKV + KL], rs_in[:, 1:2], g_ckv, ALU.mult, ALU.mult))
                    kr = cn[m % 2][:, KL:]
                    link(dve.tensor_copy(kr, z[:, Z_KR:Z_KR + ROPE]))
                    rotate(kr, n, 0, ropet[:, 0:ROPE])().then_inc(cn_ok, 1)
                elif what == "qsum":
                    dve.wait_ge(q_sq, n + 1)
                    dve.wait_ge(kv_rstd, NC + n - 1)
                    dve.tensor_reduce(st_qk[(NC + n) % 2][:, 0:8], sqq, AX, ALU.add).then_inc(qs_ok, 1)
                    dve.wait_ge(qs_ok, n + 1)
                elif what == "ksum":
                    kv_sums(n)
                elif what == "kq":
                    kv_norm(n)
                    n -= NC
                    link(TT(qk, qk, bc(rs_qk[(NC + n) % 2][:, 0:8], [P, HA, QK]), ALU.mult))
                    rotate(qk[:, :, NOPE:], n, HA, sqq[:, :, 0:ROPE])().then_inc(q_ok, 1)
                elif what == "nm":
                    o = wait_full(dve, key)
                    wait_read(dve, ("gt", n))
                    if n:
                        dve.wait_ge(hs_ok, n)
                        wait_full(dve, ("nb", n - 1))
                    done_read(TT(Dm, o.rearrange("p (a b) -> p a b", b=P), bc(gt[:, 0:HM], [P, HM, P]), ALU.add), key)
                    wait_read(dve, key)
                    TT(Dm, Dm, bc1(chunk_mask, [P, HM, P]), ALU.add).then_inc(d_ok, 1)
                elif what == "kbT":
                    o = wait_full(dve, key)
                    done_read(dve.tensor_copy(kbT, o.rearrange("p (a b) -> p a b", b=P)), key)
                    dve.wait_ge(packed, 5 * (n + 1))
                    if n:
                        wait_full(dve, ("ub", n - 1))
                    TT(kw, kb, bc(gt[:, 64:64 + HM], [P, HM, P]), ALU.mult).then_inc(kw_ok, 1)
                elif what == "qkm":
                    o = wait_full(dve, key)
                    dve.wait_ge(e_ok, n + 1)
                    done_read(TT(Dm, Dm, o.rearrange("p (a b) -> p a b", b=P), ALU.mult), key)
                elif what in ("ua", "ub"):
                    o = wait_full(dve, key)
                    cur, nxt = state[n % 2], state[(n + 1) % 2]
                    h0 = 0 if what == "ua" else 2
                    if n:
                        wait_read(dve, ("ub", n - 1))
                    if n == 1:
                        dve.wait_ge(state_out, 16)
                    mid = cur if n else nxt
                    for h in range(h0, h0 + 2):
                        u = o[:, (h - h0) * CAUG:(h - h0 + 1) * CAUG]
                        dec = decb[0:DK, h * NCH + 2 * n:h * NCH + 2 * n + 1]
                        STT(mid[DK:P, h], cur[0:DK, h], dec, u[0:DK], ALU.mult, ALU.add).then_inc(st1_ok, 1)
                    dve.wait_ge(st1_ok, HM * n + h0 + 2)
                    for h in range(h0, h0 + 2):
                        u = o[:, (h - h0) * CAUG:(h - h0 + 1) * CAUG]
                        dec = decb[DK:P, h * NCH + 2 * n + 1:h * NCH + 2 * n + 2]
                        ins = STT(nxt[0:DK, h], cur[DK:P, h], dec, u[DK:P], ALU.mult, ALU.add)
                    done_read(ins, key)
                elif what in ("ia", "ib"):
                    o = wait_full(dve, key)
                    h0 = 0 if what == "ia" else 2
                    view = o[:, 0:2 * CAUG].rearrange("p (a b) -> p a b", b=CAUG)
                    if what == "ia" and n:
                        dve.wait_ge(h_ok, n)
                    done_read(TT(num[:, h0:h0 + 2], view, bc(gt[:, 32 + h0:34 + h0], [P, 2, CAUG]), ALU.mult), key)
                    wait_read(dve, key)
                elif what in ("na", "nb"):
                    o = wait_full(dve, key)
                    h0 = 0 if what == "na" else 2
                    view = o[:, 0:2 * CAUG].rearrange("p (a b) -> p a b", b=CAUG)
                    done_read(TT(num[:, h0:h0 + 2], num[:, h0:h0 + 2], view, ALU.add), key)
                    if what == "nb":
                        mlstm_ratio(n)
                elif what == "hsq":
                    dve.wait_ge(hsq_ok, n + 1)
                    dve.tensor_reduce(st_m, Dm, AX, ALU.add).then_inc(hs_ok, 1)
                    dve.wait_ge(og_ok, n + 1)
                    link(STT(og, og, 1.0, g_mh, ALU.add, ALU.mult))
                elif what == "hout":
                    dve.wait_ge(hr_ok, n + 1)
                    link(TT(hm, hm, bc(rs_m, [P, HM, DV]), ALU.mult))
                    if n:
                        wait_full(dve, ("mxb", n - 1))
                    STT(mix[:, BANK:], hm.rearrange("p a b -> p (a b)"), 0.5, og, ALU.mult,
                        ALU.mult).then_inc(mm_ok, 1)
                elif what == "mxb":
                    o = wait_full(dve, key)
                    if n:
                        wait_full(dve, ("lg", n - 1))
                    done_read(dve.tensor_copy(mixT[:, 4:8], o.rearrange("p (a b) -> p a b", b=P)), key)
                elif what in ("o0", "o1"):
                    o = wait_full(dve, key)
                    dve.wait_ge(xres_in, 16 * (n + 1))
                    lo = 0 if what == "o0" else BANK
                    done_read(TT(xres[:, lo:lo + BANK], xres[:, lo:lo + BANK], o, ALU.add), key)
                elif what == "xnorm":
                    dve.wait_ge(x1_rs, n + 1)
                    STT(xn, xres, rs_x, g_ffn, ALU.mult, ALU.mult).then_inc(xn_ok, 1)
                elif what == "xnb":
                    o = wait_full(dve, key)
                    wait_full(dve, ("o1", n))
                    done_read(dve.tensor_copy(xnT[:, 4:8], o.rearrange("p (a b) -> p a b", b=P)), key)
                elif what == "lg":
                    o = wait_full(dve, key)
                    done_read(TT(logits[:, n], o[:, 0:NG + NE], b_route, ALU.add), key)

            def mlstm_ratio(n):
                wait_read(dve, ("na", n))
                wait_read(dve, ("nb", n))
                link(STT(den[:, 0:HM], num[:, :, DV], -1.0, num[:, :, DV], ALU.mult, ALU.max))
                link(TT(den[:, 0:HM], den[:, 0:HM], gt[:, 96:96 + HM], ALU.max))
                link(dve.reciprocal(den[:, HM:], den[:, 0:HM]))
                if n:
                    dve.wait_ge(mm_ok, n)
                TT(hm, num[:, :, 0:DV], bc(den[:, HM:], [P, HM, DV]), ALU.mult).then_inc(h_ok, 1)

            def row_max(n, h):
                q = DEC if n == 0 else P
                last = key_blocks(n)[-1]
                dve.wait_ge(s_full, 4 + n * HA + h)
                o = bank(0, 3)
                if n:
                    link(dve.memset(o[0:CH, last[0] - CH:last[0]], NEG))
                dve.tensor_reduce(nmax[0:q, h:h + 1], o[0:q, 0:last[0] + last[3]], AX, ALU.max,
                                  negate=True).then_inc(max_ok, 1)

            def pT_take(n, h):
                q = DEC if n == 0 else P
                blocks = key_blocks(n)
                for g in range(0, (len(blocks) + 3) // 4, 2):
                    key = ("pT", n, h, g)
                    o = wait_full(dve, key)
                    wait_values(dve, n, h)
                    take_pT(dve.tensor_copy, o, blocks[4 * g:4 * g + 4], 4 * g, q, key)

            def attention_out(n):
                q = DEC if n == 0 else P
                dve.wait_ge(s_read, 3 + (n + 1) * HA)
                link(dve.reciprocal(rinv[0:q], rsum[0:q]))
                dve.wait_ge(pv_done, (n + 1) * HA)
                if n:
                    wait_full(dve, ("mxb", n - 1))
                TT(mix[0:q, 0:BANK].rearrange("p (h d) -> p h d", d=VD),
                   bank(4)[0:q].rearrange("p (h d) -> p h d", d=VD), bc(rinv[0:q], [q, HA, VD]),
                   ALU.mult).then_inc(o_read, 1)

            iota, over_j = route_rows[:, 0:P], route_rows[:, P + NE:P + NE + MAX_OVER]
            from_last, at = route_rows[:, P:P + NE], P + NE + MAX_OVER
            token, nowhere = route_rows[:, at:at + NT], route_rows[:, at + NT:at + 2 * NT]
            R = rt
            col = lambda i: R["cols"][:, i]
            e32 = [P, NT, NE]

            def route_tokens(lo, hi):
                k = hi - lo
                at_ = lambda name: R[name][:, lo:hi]
                c = lambda i: R["cols"][:, i, lo:hi]

                def pick_first(scores_, top, width, one_hot, place):
                    shape = [P, k, width]
                    link(TT(one_hot, scores_, bc(top, shape), ALU.is_equal))
                    link(STT(one_hot, one_hot, -64.0, bc1(iota[:, 0:width], shape), ALU.mult, ALU.add))
                    link(dve.tensor_reduce(place, one_hot, AX, ALU.min))
                    link(TT(one_hot, one_hot, bc(place, shape), ALU.is_equal))

                gl, el = logits[:, lo:hi, 0:NG], at_("el")
                link(dve.tensor_reduce(c(0), gl, AX, ALU.max))
                pick_first(gl, c(0), NG, at_("goh"), c(15))
                link(TT(at_("ge"), gl, bc(c(0), [P, k, NG]), ALU.subtract))
                link(TS(at_("goh"), at_("goh"), -NEG, NEG, ALU.mult, ALU.add))
                link(TT(el.rearrange("p n (g e) -> p n g e", e=EG),
                        logits[:, lo:hi, NG:].rearrange("p n (g e) -> p n g e", e=EG),
                        bc(at_("goh"), [P, k, NG, EG]), ALU.add))
                link(dve.tensor_reduce(c(1), el, AX, ALU.max))
                pick_first(el, c(1), NE, at_("oh1"), c(16))
                link(STT(el, at_("oh1"), 2e8 * NEG, el, ALU.mult, ALU.add))
                link(dve.tensor_reduce(c(2), el, AX, ALU.max))
                pick_first(el, c(2), NE, at_("oh2"), c(17))
                link(TT(c(6), c(2), c(1), ALU.subtract))
                if lo == 0:
                    for oh in ("oh1", "oh2"):
                        link(dve.memset(R[oh][DEC:P, 0], 0.0))
                    link(dve.memset(R["mp"][:, 0], 0.0))
                link(TT(at_("m"), at_("oh1"), at_("oh2"), ALU.add))
                for n in range(lo, hi):
                    ins = TT(R["mp"][:, n + 1], R["mp"][:, n], R["m"][:, n], ALU.add)
                    if n < NT - 1:
                        link(ins)
                return ins

            dve.wait_ge(wuq_in, 32)
            for n in range(-1, NT + 1):
                now = 0 <= n < NT
                if n == 0:
                    gates_decays()
                if now:
                    row_max(n, 0)
                for h in range(HA):
                    if (n, h) == (0, 0):
                        dve.wait_ge(wout_in, 16 * 6)
                        link(dve.memset(mix[DEC:P, 0:BANK], 0.0))
                    if (n, h) == (-1, 2):
                        gates_log()
                    if (n, h) == (-1, 4):
                        gates_max()
                    if (n, h) == (-1, 6):
                        gates_rows()
                    if (n, h) == (-1, 7):
                        gates_end()
                    if (n, h) == (NT, 1):
                        wait_read(dve, ("lg", NT - 2))
                        route_tokens(0, NT - 1)
                    for key in filler(n, h):
                        fill_work(key)
                    if now:
                        pT_take(n, h)
                        if h + 1 < HA:
                            row_max(n, h + 1)
                for key in filler(n, HA):
                    fill_work(key)
                if now:
                    attention_out(n)

            wait_read(dve, ("lg", NT - 1))
            route_tokens(NT - 1, NT).then_inc(r_dve, 1)
            dve.wait_ge(r_act, 2)
            link(dve.tensor_reduce(col(3), R["ge"], AX, ALU.add))
            link(TS(col(4), col(6), 1.0, None, ALU.add))
            link(TT(col(5), col(3), col(4), ALU.mult))
            link(dve.reciprocal(col(7), col(5)))
            link(TT(col(8), col(7), col(6), ALU.mult))
            dve.wait_ge(r_pe, 1)
            link(dve.tensor_copy(R["rank"], bank(0)[:, 0:NT * NE].rearrange("p (a b) -> p a b", b=NE)))
            link(dve.tensor_copy(R["cnt"], bank(1)[:, 0:NE]))
            link(TS(R["ov"], R["cnt"], float(P), None, ALU.is_gt))
            for k in range(2, (TOKENS + P - 1) // P):
                link(STT(R["ov"], R["cnt"], float(k * P), R["ov"], ALU.is_gt, ALU.add))
            link(dve.memset(R["base"], 1.0))
            link(dve.tensor_tensor_scan(R["ovend"], R["base"], R["ov"], 0.0, ALU.mult, ALU.add))
            link(TT(R["base"], R["ovend"], R["ov"], ALU.subtract))
            link(TT(R["base"], R["base"], from_last, ALU.add))
            cols2 = lambda i: R["cols"][:, i:i + 2]
            rank, full_blocks, jump, place, block = cols2(9), cols2(11), cols2(13), cols2(16), cols2(18)
            for k, oh in enumerate(("oh1", "oh2")):
                for table, i in ((R["rank"], 9), (bc1(R["base"], e32), 13)):
                    link(TT(R["t"], R[oh], table, ALU.mult))
                    link(dve.tensor_reduce(col(i + k), R["t"], AX, ALU.add))
            link(TS(full_blocks, rank, float(P), None, ALU.is_ge))
            for k in range(2, (TOKENS + P - 1) // P):
                link(STT(full_blocks, rank, float(k * P), full_blocks, ALU.is_ge, ALU.add))
            link(STT(rank, full_blocks, -float(P), rank, ALU.mult, ALU.add))
            link(TS(block, full_blocks, 0.5, None, ALU.is_ge))
            link(TT(block, block, jump, ALU.mult))
            link(TT(block, block, full_blocks, ALU.add))
            link(STT(block, place, 64.0, block, ALU.add, ALU.add))
            link(TT(block, block, bc1(nowhere, [P, 2, NT]), ALU.add))
            for k in range(2):
                part = slice(k * NT, (k + 1) * NT)
                hot, toks, gates = [R["blocks"][:, part, i * NBLK:(i + 1) * NBLK] for i in range(3)]
                shape = [P, NT, NBLK]
                link(TT(R["rows"][:, part], bc1(iota, [P, NT, P]), bc(col(9 + k), [P, NT, P]), ALU.is_equal))
                link(TT(hot, bc1(iota[:, 0:NBLK], shape), bc(col(18 + k), shape), ALU.is_equal))
                link(TT(toks, hot, bc(token, shape), ALU.mult))
                TT(gates, hot, bc(col(7 + k), shape), ALU.mult).then_inc(hot_ok, 1)
            cmp = R["cmp"][0:1]
            shape = [1, MAX_OVER, NE]
            link(TT(cmp, bc1(R["ovend"][0:1], shape), bc(over_j[0:1], shape), ALU.is_le))
            link(dve.tensor_reduce(R["over"][0:1, 0:MAX_OVER], cmp, AX, ALU.add))
            link(TS(R["over"][0:1, 0:MAX_OVER], R["over"][0:1, 0:MAX_OVER], float(NE - 1), None, ALU.min))
            link(dve.tensor_copy(R["over"][0:1, MAX_OVER:], R["ovend"][0:1, NE - 1:NE]))
            link(dve.tensor_copy(over_e[:], R["over"][0:1]))
            dve.wait_ge(x1_out, 16 * NT)
            dve.wait_ge(xn_out, 16 * NT)
            dve.wait_ge(r_pe, 2)
            found, toks, gates = [bank(2)[:, i * NBLK:(i + 1) * NBLK] for i in range(3)]
            link(dve.tensor_copy(slot_tok[:], toks))
            link(dve.tensor_copy(slot_gate[:], gates))
            link(TS(R["out"], found, -NOWHERE, NOWHERE, ALU.mult, ALU.add))
            link(TT(R["out"], R["out"], toks, ALU.add))
            dve.tensor_copy(slot_out[:], R["out"]).then_inc(tab_ok, 1)

            def xeT_take(s, b):
                dve.wait_ge(xeT_full, b + 1)
                dve.tensor_copy(xeT[s], bank(0, 2).rearrange("p (k t) -> p k t", t=P)).then_inc(xeT_read, 1)

            def silu(b):
                dve.wait_ge(tanh_ok, b + 1)
                STT(uu, th, 1.0, bank(2), ALU.add, ALU.mult).then_inc(u_ok, 1)

            def hidden(b):
                dve.wait_ge(u_ok, b + 1)
                dve.wait_ge(h3_full, b + 1)
                dve.wait_ge(hT_full, b)
                STT(hh, uu, 0.5, bank(3), ALU.mult, ALU.mult).then_inc(hh_ok, 1)

            def hT_take(b):
                dve.wait_ge(hT_full, b + 1)
                dve.wait_ge(y_full, b)
                dve.tensor_copy(hT, bank(4).rearrange("p (k t) -> p k t", t=P)).then_inc(hT_read, 1)

            xeT_take(0, 0)
            silu(0)
            xeT_take(1, 1)
            hidden(0)
            with dve.Fori(0, NE // 2 - 1) as j:
                for i in range(2):
                    b, s = 2 * j + 1 + i, 1 - i
                    hT_take(b - 1)
                    silu(b)
                    xeT_take(1 - s, b + 1)
                    hidden(b)
            hT_take(NE - 2)
            silu(NE - 1)
            hidden(NE - 1)
            hT_take(NE - 1)
            total = dve.value_load(over_e[0:1, MAX_OVER:MAX_OVER + 1], min_val=0, max_val=MAX_OVER)
            with dve.If(total > 0):
                with dve.Fori(0, MAX_OVER) as j:
                    with dve.If(j < total):
                        xeT_take(0, NE + j)
                        silu(NE + j)
                        hidden(NE + j)
                        hT_take(NE + j)


def kernel(**inputs):
    import numpy as _np
    import concourse.bacc as _bacc
    from concourse.bass_utils import run_bass_kernel_spmd as _run

    a = {k: _np.asarray(v)[0] if k not in ("x_prompt", "x_sample", "meta_tokens") else _np.asarray(v)
         for k, v in inputs.items()}
    x = _np.zeros((ROWS, D), _np.float32)
    x[:DEC] = a["x_sample"][0]
    x[DEC:DEC + META] = a["meta_tokens"]
    x[P:] = a["x_prompt"][0]
    w = a["w_in"]
    gates = QL + KL + ROPE + 2 * HM * DK + HM * DV
    first = QL + KL + ROPE
    cols = [w[:, :first], w[:, gates:gates + 2 * HM], w[:, first:gates], w[:, gates + 2 * HM:]]
    ukv = a["w_ukv"].reshape(KL, HA, NOPE + VD)
    host = {
        "x_rows": x,
        "cache_ckv": a["cache_ckv"][0],
        "cache_kr": a["cache_krope"][0],
        "state_c": _np.concatenate([a["state_mlstm_c"][0].transpose(2, 0, 1),
                                    a["state_mlstm_n"][0].T[:, :, None]], axis=2).reshape(DK, HM * CAUG),
        "state_m": a["state_mlstm_m"].reshape(HM, 1),
        "g_attn": a["g_attn"].reshape(KD, P).T,
        "w_in": _np.concatenate(cols, axis=1),
        "g_cq": a["g_cq"].reshape(QL // P, P).T,
        "w_uq": a["w_uq"].reshape(QL, HA * QK),
        "g_ckv": a["g_ckv"][None],
        "w_ukv": _np.concatenate([ukv[:, :, :NOPE].reshape(KL, -1), ukv[:, :, NOPE:].reshape(KL, -1)], axis=1),
        "g_q": a["g_q"][:, None],
        "g_k": a["g_k"][:, None],
        "b_gate": _np.stack([a["b_igate"], a["b_fgate"]], axis=1),
        "g_mh": a["g_mh"].reshape(1, HM * DV),
        "w_out": a["w_out"],
        "g_ffn": a["g_ffn"][None],
        "w_route": _np.concatenate([a["w_group"], a["w_erouter"]], axis=1),
        "b_route": _np.concatenate([a["b_group"], a["b_erouter"]])[None],
        "w1": a["w1"], "w3": a["w3"], "w2": a["w2"],
    }
    nc = _bacc.Bacc("TRN2", target_bir_lowering=False, num_devices=1)
    T, O, arrays = {}, {}, {}
    for name, array in {**host, **CONSTS}.items():
        array = _np.ascontiguousarray(array)
        assert array.shape == INS.get(name, array.shape), (name, array.shape)
        arrays["in_" + name] = array
        T[name] = nc.dram_tensor("in_" + name, array.shape, mybir.dt.from_np(array.dtype), kind="ExternalInput").ap()
    for name, shape in OUTS.items():
        O[name] = nc.dram_tensor("out_" + name, shape, F32, kind="ExternalOutput").ap()
    build(nc, T, O)
    r = _run(nc, [arrays], core_ids=[0]).results[0]
    o = {name: _np.asarray(r["out_" + name]) for name in OUTS}

    def state_of(s):
        s = s.reshape(DK, HM, CAUG).transpose(1, 2, 0)
        return s[None, None, :, :DV], s[None, None, :, DV]

    c_p, n_p = state_of(o["c_prompt"])
    c_s, n_s = state_of(o["c_sample"])
    return (o["y"][None, P:], o["y"][None, :DEC], o["ckv"][None, None, DEC:][:, :, list(range(META)) + list(range(P - DEC, ROWS - DEC))],
            o["krope"][None, None, DEC:][:, :, list(range(META)) + list(range(P - DEC, ROWS - DEC))], c_p, n_p,
            o["m_both"][None, None, 0, :, 0], o["ckv"][None, None, :DEC], o["krope"][None, None, :DEC], c_s, n_s,
            o["m_both"][None, None, 1, :, 0])
```
